# Optimizing a Trainium2 kernel written in Bass

```python
import math
import jax, jax.numpy as jnp
from jax import lax
import numpy as np

D_MODEL = 1024
BATCH = 1
SEQ = 256
DEPTH = 2

DIFF_HEADS = 4
DIFF_QK_DIM = 64
DIFF_V_DIM = 2 * DIFF_QK_DIM
DIFF_WIDTH = DIFF_HEADS * DIFF_V_DIM
MLA_HEADS = 8
MLA_NOPE_DIM = 64
MLA_ROPE_DIM = 32
MLA_V_DIM = 64
MLA_Q_RANK = 384
MLA_KV_RANK = 256
MLA_WIDTH = MLA_HEADS * MLA_V_DIM
MIX_WIDTH = DIFF_WIDTH + MLA_WIDTH
ROPE_THETA = 10000.0
IN_DQ = DIFF_HEADS * 2 * DIFF_QK_DIM
IN_DK = DIFF_HEADS * 2 * DIFF_QK_DIM
IN_DV = DIFF_WIDTH
IN_MQ = MLA_Q_RANK
IN_MKV = MLA_KV_RANK + MLA_ROPE_DIM
IN_WIDTH = IN_DQ + IN_DK + IN_DV + IN_MQ + IN_MKV
N_BUCKETS = 32
MAX_EXACT = 16
MAX_DISTANCE = 128
D_FF = 2816
N_EXPERTS = 8
TOP_K = 2
Q_BLOCK = 128
NORM_EPS = 1e-6
ADA_CHUNKS = 6

kernel_name = 'hybrid_diffattn_mla_moe_adaln'

def rms_norm(x, g):
    xf = x.astype(jnp.float32)
    y = xf * lax.rsqrt(jnp.mean(xf * xf, axis=-1, keepdims=True) + NORM_EPS)
    return (y * g.astype(jnp.float32)).astype(x.dtype)

def rel_bucket(dist):
    n = jnp.maximum(dist, 0)
    nf = jnp.maximum(n, 1).astype(jnp.float32)
    large = MAX_EXACT + (jnp.log(nf / MAX_EXACT) / math.log(MAX_DISTANCE / MAX_EXACT)
                         * (N_BUCKETS - MAX_EXACT)).astype(jnp.int32)
    large = jnp.minimum(large, N_BUCKETS - 1)
    return jnp.where(n < MAX_EXACT, n, large)

def rope(x, positions):
    half = MLA_ROPE_DIM // 2
    inv_freq = ROPE_THETA ** (-jnp.arange(half, dtype=jnp.float32) / half)
    ang = positions.astype(jnp.float32)[..., None] * inv_freq
    ang = ang.reshape(ang.shape[:2] + (1,) * (x.ndim - 3) + (half,))
    cos = jnp.cos(ang).astype(x.dtype)
    sin = jnp.sin(ang).astype(x.dtype)
    x1, x2 = x[..., :half], x[..., half:]
    return jnp.concatenate([x1 * cos - x2 * sin, x2 * cos + x1 * sin], axis=-1)

def diff_attention(q, k, v, lam, positions, rel_bias):
    s = q.shape[1]
    scale = DIFF_QK_DIM ** -0.5
    outs = []
    for i in range(s // Q_BLOCK):
        q0, q1 = i * Q_BLOCK, (i + 1) * Q_BLOCK
        qb, kp, vp = q[:, q0:q1], k[:, :q1], v[:, :q1]
        dist = positions[:, q0:q1, None] - positions[:, None, :q1]
        bias = jnp.transpose(rel_bias[rel_bucket(dist)], (0, 3, 1, 2)).astype(jnp.float32)
        causal = jnp.arange(q0, q1)[:, None] >= jnp.arange(q1)[None, :]
        logits = jnp.einsum('bqhmd,bkhmd->bhmqk', qb, kp).astype(jnp.float32) * scale + bias[:, :, None]
        logits = jnp.where(causal, logits, -jnp.inf)
        p = jax.nn.softmax(logits, axis=-1)
        a = p[:, :, 0] - lam * p[:, :, 1]
        outs.append(jnp.einsum('bhqk,bkhd->bqhd', a.astype(v.dtype), vp))
    return jnp.concatenate(outs, axis=1)

def mla_attention(q_nope, q_rope, k_nope, k_rope, v):
    s = q_nope.shape[1]
    scale = (MLA_NOPE_DIM + MLA_ROPE_DIM) ** -0.5
    outs = []
    for i in range(s // Q_BLOCK):
        q0, q1 = i * Q_BLOCK, (i + 1) * Q_BLOCK
        causal = jnp.arange(q0, q1)[:, None] >= jnp.arange(q1)[None, :]
        logits = (jnp.einsum('bqhd,bkhd->bhqk', q_nope[:, q0:q1], k_nope[:, :q1])
                  + jnp.einsum('bqhr,bkr->bhqk', q_rope[:, q0:q1], k_rope[:, :q1])).astype(jnp.float32) * scale
        logits = jnp.where(causal, logits, -jnp.inf)
        p = jax.nn.softmax(logits, axis=-1)
        outs.append(jnp.einsum('bhqk,bkhd->bqhd', p.astype(v.dtype), v[:, :q1]))
    return jnp.concatenate(outs, axis=1)

def token_mixer(h, positions, layer, w_in, diff_lambda, diff_subln_g, rel_bias,
                mla_q_norm, w_uq, mla_kv_norm, w_ukv, w_o):
    b, s, _ = h.shape
    proj = h @ w_in
    cuts = [IN_DQ, IN_DQ + IN_DK, IN_DQ + IN_DK + IN_DV, IN_DQ + IN_DK + IN_DV + IN_MQ]
    dq, dk, dv, mq, mkv = jnp.split(proj, cuts, axis=-1)
    lam_init = 0.8 - 0.6 * math.exp(-0.3 * layer)
    lv = diff_lambda.astype(jnp.float32)
    lam = jnp.exp(jnp.sum(lv[0] * lv[1])) - jnp.exp(jnp.sum(lv[2] * lv[3])) + lam_init
    o_diff = diff_attention(dq.reshape(b, s, DIFF_HEADS, 2, DIFF_QK_DIM),
                            dk.reshape(b, s, DIFF_HEADS, 2, DIFF_QK_DIM),
                            dv.reshape(b, s, DIFF_HEADS, DIFF_V_DIM),
                            lam, positions, rel_bias)
    o_diff = (rms_norm(o_diff, diff_subln_g) * (1.0 - lam_init)).reshape(b, s, DIFF_WIDTH)
    q = (rms_norm(mq, mla_q_norm) @ w_uq).reshape(b, s, MLA_HEADS, MLA_NOPE_DIM + MLA_ROPE_DIM)
    q_nope = q[..., :MLA_NOPE_DIM]
    q_rope = rope(q[..., MLA_NOPE_DIM:], positions)
    kv = (rms_norm(mkv[..., :MLA_KV_RANK], mla_kv_norm) @ w_ukv).reshape(b, s, MLA_HEADS, MLA_NOPE_DIM + MLA_V_DIM)
    k_nope, v = kv[..., :MLA_NOPE_DIM], kv[..., MLA_NOPE_DIM:]
    k_rope = rope(mkv[..., MLA_KV_RANK:], positions)
    o_mla = mla_attention(q_nope, q_rope, k_nope, k_rope, v).reshape(b, s, MLA_WIDTH)
    return jnp.concatenate([o_diff, o_mla], axis=-1) @ w_o

def swiglu(h, w1, w3, w2):
    return (jax.nn.silu(h @ w1) * (h @ w3)) @ w2

def moe_ffn(h, w_router, w1, w3, w2):
    logits = (h @ w_router).astype(jnp.float32)
    top_v, top_i = lax.top_k(logits, TOP_K)
    top_w = jax.nn.softmax(top_v, axis=-1)
    gates = jnp.sum(jax.nn.one_hot(top_i, N_EXPERTS, dtype=jnp.float32) * top_w[..., None], axis=-2)
    y = jnp.zeros_like(h)
    for e in range(N_EXPERTS):
        y = y + gates[..., e:e + 1].astype(h.dtype) * swiglu(h, w1[e], w3[e], w2[e])
    return y

def setup_inputs(seed: int = 0) -> dict:
    key = jax.random.key(seed)
    ks = jax.random.split(key, 32)
    n_dense = (DEPTH + 1) // 2
    n_moe = DEPTH // 2
    f32 = jnp.float32

    def nrm(k, shape, scale):
        return jax.random.normal(k, shape, f32) * scale

    def gain(k, shape):
        return 1.0 + 0.01 * jax.random.normal(k, shape, f32)

    x = jax.random.normal(ks[0], (BATCH, SEQ, D_MODEL), f32)
    c = jax.random.normal(ks[1], (BATCH, D_MODEL), f32)
    offsets = jax.random.randint(ks[2], (BATCH, 1), 0, 4096, dtype=jnp.int32)
    positions = offsets + jnp.arange(SEQ, dtype=jnp.int32)[None, :]
    return {
        'x': x,
        'c': c,
        'positions': positions,
        'w_ada': nrm(ks[3], (DEPTH, D_MODEL, ADA_CHUNKS * D_MODEL), 0.1 * D_MODEL ** -0.5),
        'b_ada': nrm(ks[4], (DEPTH, ADA_CHUNKS * D_MODEL), 0.01),
        'g_attn': gain(ks[5], (DEPTH, D_MODEL)),
        'w_in': nrm(ks[6], (DEPTH, D_MODEL, IN_WIDTH), D_MODEL ** -0.5),
        'diff_lambda': nrm(ks[7], (DEPTH, 4, DIFF_QK_DIM), 0.1),
        'diff_subln_g': gain(ks[8], (DEPTH, DIFF_V_DIM)),
        'rel_bias': nrm(ks[9], (N_BUCKETS, DIFF_HEADS), 0.5),
        'mla_q_norm': gain(ks[10], (DEPTH, MLA_Q_RANK)),
        'w_uq': nrm(ks[11], (DEPTH, MLA_Q_RANK, MLA_HEADS * (MLA_NOPE_DIM + MLA_ROPE_DIM)), MLA_Q_RANK ** -0.5),
        'mla_kv_norm': gain(ks[12], (DEPTH, MLA_KV_RANK)),
        'w_ukv': nrm(ks[13], (DEPTH, MLA_KV_RANK, MLA_HEADS * (MLA_NOPE_DIM + MLA_V_DIM)), MLA_KV_RANK ** -0.5),
        'w_o': nrm(ks[14], (DEPTH, MIX_WIDTH, D_MODEL), MIX_WIDTH ** -0.5),
        'g_ffn': gain(ks[15], (DEPTH, D_MODEL)),
        'ffn_w1': nrm(ks[16], (n_dense, D_MODEL, D_FF), D_MODEL ** -0.5),
        'ffn_w3': nrm(ks[17], (n_dense, D_MODEL, D_FF), D_MODEL ** -0.5),
        'ffn_w2': nrm(ks[18], (n_dense, D_FF, D_MODEL), D_FF ** -0.5),
        'moe_router': nrm(ks[19], (n_moe, D_MODEL, N_EXPERTS), D_MODEL ** -0.5),
        'moe_w1': nrm(ks[20], (n_moe, N_EXPERTS, D_MODEL, D_FF), D_MODEL ** -0.5),
        'moe_w3': nrm(ks[21], (n_moe, N_EXPERTS, D_MODEL, D_FF), D_MODEL ** -0.5),
        'moe_w2': nrm(ks[22], (n_moe, N_EXPERTS, D_FF, D_MODEL), D_FF ** -0.5),
        'g_final': gain(ks[23], (D_MODEL,)),
    }

def reference(x, c, positions, w_ada, b_ada, g_attn, w_in, diff_lambda, diff_subln_g, rel_bias,
              mla_q_norm, w_uq, mla_kv_norm, w_ukv, w_o, g_ffn, ffn_w1, ffn_w3, ffn_w2,
              moe_router, moe_w1, moe_w3, moe_w2, g_final):
    cond = jax.nn.silu(c)
    for l in range(DEPTH):
        mod = cond @ w_ada[l] + b_ada[l]
        sh_a, sc_a, gt_a, sh_f, sc_f, gt_f = jnp.split(mod[:, None, :], ADA_CHUNKS, axis=-1)
        h = rms_norm(x, g_attn[l]) * (1.0 + sc_a) + sh_a
        x = x + (1.0 + gt_a) * token_mixer(h, positions, l, w_in[l], diff_lambda[l], diff_subln_g[l],
                                           rel_bias, mla_q_norm[l], w_uq[l], mla_kv_norm[l],
                                           w_ukv[l], w_o[l])
        h = rms_norm(x, g_ffn[l]) * (1.0 + sc_f) + sh_f
        if l % 2 == 0:
            y = swiglu(h, ffn_w1[l // 2], ffn_w3[l // 2], ffn_w2[l // 2])
        else:
            y = moe_ffn(h, moe_router[l // 2], moe_w1[l // 2], moe_w3[l // 2], moe_w2[l // 2])
        x = x + (1.0 + gt_f) * y
    return rms_norm(x, g_final)


_drawn_inputs = setup_inputs


def setup_inputs(seed=0):
    import zlib

    import numpy as np

    out = dict(_drawn_inputs(seed))
    spreads = {}
    factors = {'mla_q_norm': 8.0,
     'mla_kv_norm': 8.0,
     'g_ffn': 2.883,
     'g_final': 34.078,
     'diff_subln_g': 3.05}
    for name, (base, spread) in spreads.items():
        noise = np.random.default_rng([zlib.crc32(name.encode()), seed]).standard_normal(out[name].shape)
        drawn = base * np.exp(spread * noise) if base else spread * noise
        out[name] = __import__('jax').numpy.asarray(drawn.astype(out[name].dtype))
    for name, factor in factors.items():
        out[name] = (out[name] * factor).astype(out[name].dtype)
    return out
```

```python
import math
from contextlib import ExitStack

import concourse.bass as bass
from concourse import mybir

F32 = mybir.dt.float32
F32R = mybir.dt.float32r
I32 = mybir.dt.int32
U32 = mybir.dt.uint32
ALU = mybir.AluOpType
ACT = mybir.ActivationFunctionType
AX = mybir.AxisListType

P = 128
D = 1024
SEQ = 256
TILES = SEQ // P
KC = D // P
DEPTH = 2
DIFF_HEADS = 4
MLA_HEADS = 8
QK = 64
ROPE = 32
HALF = ROPE // 2
MD = QK + ROPE
Q_RANK = 384
KV_RANK = 256
MKV = KV_RANK + ROPE
BUCKETS = 32
D_FF = 2816
FB = 256
BLOCKS = D_FF // FB
EXPERTS = 8
SLOTS = P
MAX_OVER = (2 * SEQ) // (SLOTS + 1)
MAX_PASS = EXPERTS + MAX_OVER
EPS = 1e-6
MASKED = -1e30
NB = 512
UNIT = 2048
RAW = 11
HIS = 3
THETA = 10000.0
LAM_INIT = [0.8 - 0.6 * math.exp(-0.3 * l) for l in range(DEPTH)]
THRESHOLDS = list(range(1, 17)) + [math.ceil(16 * 8 ** ((b - 16) / 16) - 1e-9) for b in range(17, BUCKETS)]

IN_GROUPS = [("mq", 1536, Q_RANK), ("mkv", 1920, MKV), ("dq", 0, 512), ("dk", 512, 512), ("dv", 1024, 512)]


def static_units():
    units = []

    def ada(l, g):
        units.extend((("ada", l, g, kh), UNIT, False) for kh in range(2))

    for l in range(DEPTH):
        if l == 0:
            for g in range(4):
                ada(0, g)
        for gi, (_, _, w) in enumerate(IN_GROUPS):
            units.extend((("in", l, gi, kh), 4 * w, True) for kh in range(2))
        units.extend((("uq", l, u), 3 * 384, True) for u in range(2))
        units.append((("ukv", l), UNIT, True))
        for g in (range(4, 12) if l == 0 else range(10, 12)):
            ada(l, g)
        units.extend((("wo", l, nh, kh), UNIT, True) for nh in range(2) for kh in range(2))
        if l == 0:
            for j in range(BLOCKS):
                units.append((("A", j), UNIT, True))
                units.append((("B", j), UNIT, True))
                if j:
                    units.append((("C", j - 1), UNIT, True))
                if j < 10:
                    ada(1, j)
            units.append((("C", BLOCKS - 1), UNIT, True))
    return units


def ffn_order():
    out = []
    for j in range(BLOCKS):
        out += [("A", j), ("B", j)] + ([("C", j - 1)] if j else [])
    return out + [("C", BLOCKS - 1)]


CONSTS = {}
_at = 0
for _n, _w in (("ident", 128), ("mask", 384), ("before", 128), ("selrow", 128), ("iota", 128), ("freq", HALF)):
    CONSTS[_n] = (_at, _at + _w)
    _at += _w
N_CONST = _at
COLS = {}
_at = 0
for _n, _w in (("g_attn", 16), ("g_ffn", 16), ("b_ada", 96), ("q_norm", 6), ("kv_norm", 4), ("subln", 2), ("c", 8),
               ("router", 64)):
    COLS[_n] = (_at, _at + _w)
    _at += _w
N_COLS = _at


def build(nc, x_in, pos_in, pos_cols, consts_in, cols_in, b_ada, rel_bias, diff_lambda, g_final, w_static, w_moe, out):
    UN = static_units()
    N_STATIC = len(UN)
    unit_of = {name: n for n, (name, _, _) in enumerate(UN)}
    offset, at = [], 0
    for _, cols, _ in UN:
        offset.append(at)
        at += P * cols
    split_units = [n for n, u in enumerate(UN) if u[2]]
    split_of = {UN[n][0]: h for h, n in enumerate(split_units)}
    N_SPLIT = len(split_units)
    done_of, at = [], 0
    for _, _, split in UN:
        at += 2 if split else 1
        done_of.append(at)
    FFN = ffn_order()
    UPP = len(FFN)
    ffn_index = {name: r for r, name in enumerate(FFN)}
    assert UPP % RAW == 0 and UPP % HIS == 0

    with ExitStack() as ctx:
        top = [(nc.sbuf_base + 63) // 64 * 64]

        def at_offset(name, shape, dt, offset):
            return nc.alloc_sbuf_tensor_at(name, shape, dt, offset=offset).ap()

        def size(shape):
            n = 4
            for s in shape[1:]:
                n *= s
            return (n + 31) // 32 * 32

        def sb(name, shape, dt=F32):
            t = at_offset(name, shape, dt, top[0])
            top[0] += size(shape)
            return t

        raw_at = top[0]
        raw = sb("raw", [P, RAW, UNIT])
        w_lo = at_offset("w_lo", [P, RAW, UNIT], F32R, raw_at)
        w_hi = sb("w_hi", [P, HIS, UNIT], F32R)
        x = sb("x", [P, TILES, D])
        TH = sb("TH", [P, KC, SEQ], F32R)
        TL = sb("TL", [P, KC, SEQ], F32R)
        gate_a = sb("gate_a", [P, D])
        gate_f = sb("gate_f", [P, D])
        bias_at = top[0]
        bias = sb("bias", [P, DIFF_HEADS, 384])
        consts = sb("consts", [P, N_CONST])
        cols = sb("cols", [P, N_COLS])
        ones = sb("ones", [P, P])
        ada_p = sb("ada_p", [P, 2, NB])
        cond = sb("cond", [P, KC])
        cond_rep = sb("cond_rep", [P, KC, 32])
        mod = sb("mod", [P, DEPTH, 48])
        mod_a = sb("mod_a", [P, 2 * DEPTH, KC])
        h32_at = top[0]
        h32 = sb("h32", [P, 2, NB])
        tmp = at_offset("tmp", [P, 2, NB], F32, h32_at)
        rot = at_offset("rot", [P, 4, TILES * MLA_HEADS * HALF], F32, h32_at)
        ssq = sb("ssq", [P, 9, 8])
        ms = sb("ms", [P, 9, 8])
        rstd = sb("rstd", [P, 9, 8])
        neg_half = sb("neg_half", [P, 8])
        o_scale = sb("o_scale", [P, DEPTH, KC])
        lam_sum = sb("lam_sum", [P, 4])
        lam_exp = sb("lam_exp", [P, 4])
        neg_lam = sb("neg_lam", [P, DEPTH])
        pos_i = sb("pos_i", [P, 2], I32)
        posq = sb("posq", [P, 2])
        rb = sb("rb", [P, BUCKETS, DIFF_HEADS])
        rb_step = sb("rb_step", [P, BUCKETS - 1, DIFF_HEADS])
        ang = sb("ang", [P, TILES, HALF])
        turns = sb("turns", [P, TILES, HALF])
        ang_c = sb("ang_c", [P, TILES, HALF])
        cos = sb("cos", [P, TILES, HALF])
        sin = sb("sin", [P, TILES, HALF])
        neg_max = sb("neg_max", [P, 16, 2])
        psum_p = sb("psum_p", [P, 16, 2])
        rec = sb("rec", [P, 16, 2])
        rec_lam = sb("rec_lam", [P, 16, 2])
        region = top[0]

        top[0] = region
        mT_at = top[0]
        mT = sb("mT", [P, 2, 4, NB])
        xn = at_offset("xn", [P, TILES, D], F32, mT_at)
        dT = sb("dT", [P, 2, 2, NB])
        qk_at = top[0]
        qfull = sb("qfull", [P, TILES, MLA_HEADS * MD])
        kfull = sb("kfull", [P, TILES, MLA_HEADS, MD])
        o = at_offset("o", [P, TILES, D], F32, qk_at)
        posk_i = at_offset("posk_i", [P, SEQ], I32, top[0])
        vm = sb("vm", [P, TILES, NB])
        lam_rows = at_offset("lam_rows", [P, DEPTH, 4, QK], F32, top[0])
        dv = sb("dv", [P, TILES, NB])
        d_at = top[0]
        dq = sb("dq", [P, TILES, NB])
        dk = sb("dk", [P, TILES, NB])
        probs = at_offset("probs", [P, 3, 2, SEQ], F32, d_at)
        posk = at_offset("posk", [P, SEQ], F32, d_at)
        dist = at_offset("dist", [P, 384], F32, mT_at + 8192)
        far = at_offset("far", [P, 2, 384], F32, mT_at + 8192 + 1536)
        pT = [at_offset("pT0", [P, NB], F32, d_at + 6144), sb("pT1", [P, NB])]
        mq = at_offset("mq", [P, TILES, Q_RANK], F32, mT_at)
        mkv = at_offset("mkv", [P, TILES, MKV], F32, mT_at + size([P, TILES, Q_RANK]))
        end_attention = top[0]

        top[0] = region
        moe_out = sb("moe_out", [P, TILES, D])
        dense_aT = [at_offset(f"dense_aT{i}", [P, 2, 2 * SEQ], F32R, top[0] + i * 2 * 2 * SEQ * 4) for i in range(2)]
        xn_hi = sb("xn_hi", [P, TILES, D], F32R)
        xn_lo = sb("xn_lo", [P, TILES, D], F32R)
        xg32 = sb("xg32", [P, KC, SLOTS])
        xg_hi = sb("xg_hi", [P, KC, SLOTS], F32R)
        xg_lo = sb("xg_lo", [P, KC, SLOTS], F32R)
        y_hi = at_offset("y_hi", [P, D], F32R, bias_at)
        y_lo = sb("y_lo", [P, D], F32R)
        slot_of = sb("slot_of", [P, TILES, SLOTS], F32R)
        token_of = sb("token_of", [P, SEQ], F32R)
        silu = sb("silu", [P, 2, FB])
        act_f = sb("act_f", [P, 2, FB])
        expert_aT = [sb(f"expert_aT{i}", [P, 2, FB], F32R) for i in range(2)]
        aT = {1: expert_aT, 2: dense_aT}
        router_hi = sb("router_hi", [P, KC * EXPERTS], F32R)
        router_lo = sb("router_lo", [P, KC * EXPERTS], F32R)
        rl = sb("rl", [P, TILES, EXPERTS])
        top_v = sb("top_v", [P, TILES, 8])
        top_i = sb("top_i", [P, TILES, 8], U32)
        top_f = sb("top_f", [P, TILES, 8])
        top_w = sb("top_w", [P, TILES, 4])
        hot = sb("hot", [P, TILES, 2, EXPERTS])
        pos_t = sb("pos_t", [P, TILES, MAX_PASS + 1])
        sel_t = sb("sel_t", [P, TILES, MAX_PASS + 1])
        gate_t = sb("gate_t", [P, TILES, MAX_PASS + 1])
        count = sb("count", [P, EXPERTS])
        over = sb("over", [P, EXPERTS])
        rank = sb("rank", [P, EXPERTS + 1])
        over_hot = sb("over_hot", [P, MAX_OVER, EXPERTS])
        junk8 = sb("junk8", [P, 8])
        pass_f = sb("pass_f", [P, MAX_PASS + 2])
        pass_i = sb("pass_i", [P, MAX_PASS + 2], I32)
        assert max(top[0], end_attention) <= nc.sbuf_usable_end, (top[0], end_attention, nc.sbuf_usable_end)

        bank = [ctx.enter_context(nc.psum_tensor(f"bank{i}", [P, NB], F32)) for i in range(8)]
        bank = [b[:] for b in bank]
        ADA = bank[7]

        def const(name):
            return consts[:, CONSTS[name][0]:CONSTS[name][1]]

        def col(name):
            return cols[:, COLS[name][0]:COLS[name][1]]

        ident, iota = const("ident"), const("iota")
        g_attn = col("g_attn").rearrange("p (l c) -> p l c", l=DEPTH)
        g_ffn = col("g_ffn").rearrange("p (l c) -> p l c", l=DEPTH)
        b_col = col("b_ada").rearrange("p (l c) -> p l c", l=DEPTH)
        q_gain = col("q_norm").rearrange("p (l c) -> p l c", l=DEPTH)
        kv_gain = col("kv_norm").rearrange("p (l c) -> p l c", l=DEPTH)

        def sem(name):
            return ctx.enter_context(nc.semaphore(name))

        raw_loaded = [sem(f"raw_loaded{i}") for i in range(RAW)]
        x_loaded, small_loaded = sem("x_loaded"), sem("small_loaded")
        gate_a_row, gate_f_row = sem("gate_a_row"), sem("gate_f_row")
        hi_ready, lo_ready, unit_done = sem("hi_ready"), sem("lo_ready"), sem("unit_done")
        silu_c, ones_ready, cond_ready = sem("silu_c"), sem("ones_ready"), sem("cond_ready")
        lam_summed, lam_exped, angles, trig = sem("lam_summed"), sem("lam_exped"), sem("angles"), sem("trig")
        ada_part, ada_comb, ada_used = sem("ada_part"), sem("ada_comb"), sem("ada_used")
        mod_ready = sem("mod_ready")
        ssq_ready, pool_step, rstd_ready, xn_ready = sem("ssq_ready"), sem("pool_step"), sem("rstd_ready"), sem("xn_ready")
        filled, evacuated, split_t = sem("filled"), sem("evacuated"), sem("split_t")
        kn_done, acc_act, acc_dve = sem("kn_done"), sem("acc_act"), sem("acc_dve")
        roped = sem("roped")
        scored, soft, exped, recip = sem("scored"), sem("soft"), sem("exped"), sem("recip")
        pT_filled, pT_ready, pv_done, o_ready = sem("pT_filled"), sem("pT_ready"), sem("pv_done"), sem("o_ready")
        silu_done, act_done = sem("silu_done"), sem("act_done")
        aT_filled, aT_hi_ready, aT_lo_ready = sem("aT_filled"), sem("aT_hi_ready"), sem("aT_lo_ready")
        ffn_added = sem("ffn_added")
        dve_step = sem("dve_step")
        xn_split, routed, chosen, top_exp, placed_ps = (sem(n) for n in ("xn_split", "routed", "chosen", "top_exp", "placed_ps"))
        tables, slots_built, token_filled, token_ready = (sem(n) for n in ("tables", "slots_built", "token_filled", "token_ready"))
        gathered, xg_evac, xg_split = sem("gathered"), sem("xg_evac"), sem("xg_split")
        y_hi_ready, y_lo_ready, scattered, moe_added = (sem(n) for n in ("y_hi_ready", "y_lo_ready", "scattered", "moe_added"))
        moe_in_x, final_ready, stored = sem("moe_in_x"), sem("final_ready"), sem("stored")

        acc_groups = []
        for l in range(DEPTH):
            acc_groups += [("in", l, gi) for gi in range(5)] + [("uq", l, 0), ("uq", l, 1), ("kn", l), ("v", l)]
            acc_groups += [("wo", l, 0), ("wo", l, 1)]
        acc_of = {g: q for q, g in enumerate(acc_groups)}
        act_count, dve_count, acc_free = 0, 0, []
        for g in acc_groups:
            if g[0] == "wo":
                dve_count += 1
                acc_free.append((acc_dve, dve_count))
            else:
                act_count += 1
                acc_free.append((acc_act, act_count))
        fills = []
        for l in range(DEPTH):
            fills += [("h", l, i) for i in range(4)] + [("mq", l, 0), ("mq", l, 1), ("ckv", l, 0)]
            fills += [("dT", l, qk, hp) for qk in range(2) for hp in range(2)]
            fills += [("mT", l, qk, hp) for qk in range(2) for hp in range(4)]
            fills += [("o", l, i) for i in range(4)] + [("f", l, i) for i in range(4)]
        fill_of = {f: i for i, f in enumerate(fills)}
        split_fills = [f for f in fills if f[0] in ("h", "mq", "ckv", "o", "f")]
        sfill_of = {f: i for i, f in enumerate(split_fills)}
        rms = {e: i for i, e in enumerate([("h", 0), ("lat", 0), ("sub", 0), ("f", 0), ("h", 1), ("lat", 1), ("sub", 1), ("f", 1), ("final", 1)])}
        ada_groups = [(0, g) for g in range(12)] + [(1, g) for g in range(12)]
        steps = [("diff", hp, t, m) for hp in range(2) for t in range(TILES) for m in range(2)]
        steps += [("mla", hp, t, 0) for hp in range(4) for t in range(TILES)]
        NS = len(steps)

        def n_keys(s):
            return P * (steps[s][2] + 1)

        def wait(eng, s, value):
            if not isinstance(value, int) or value > 0:
                eng.wait_ge(s, value)

        class Unit:

            def __init__(self, name, p=None):
                if p is None:
                    self.n = unit_of[name]
                    self.slot, self.cols = self.n % RAW, UN[self.n][1]
                    self.loaded = 16 * (self.n // RAW + 1)
                    self.done = done_of[self.n]
                    if UN[self.n][2]:
                        h = split_of[name]
                        self.hi_slot = h % HIS
                        self.part_done = (self.done - 1, self.done)
                        self.ready = (2 * h + 1, 2 * h + 2)
                        before = done_of[split_units[h - HIS]] if h >= HIS else 0
                        self.hi_free = (before - 1, before)
                else:
                    r = name
                    n = N_STATIC + r
                    self.slot, self.cols = n % RAW, UNIT
                    self.loaded = p * (16 * UPP // RAW) + 16 * (n // RAW + 1)
                    self.done = p * (2 * UPP) + (done_of[-1] + 2 * (r + 1))
                    self.part_done = (self.done - 1, self.done)
                    h = N_SPLIT + r
                    self.hi_slot = h % HIS
                    self.ready = (p * (2 * UPP) + (2 * h + 1), p * (2 * UPP) + (2 * h + 2))
                    self.hi_free = (self.done - 2 * HIS - 1, self.done - 2 * HIS)
                cut = 2 * self.cols // 3 if p is None and name[0] == "uq" else self.cols // 2
                self.cut = cut
                self.parts = [(slice(a, b), slice(part * UNIT // 2, part * UNIT // 2 + b - a))
                              for part, (a, b) in enumerate(((0, cut), (cut, self.cols)))]

            def hi_cols(self, cs):
                shift = UNIT // 2 - self.cut if cs.start >= self.cut else 0
                return slice(cs.start + shift, cs.stop + shift)

        def act_hi(eng, u):
            eng.wait_ge(raw_loaded[u.slot], u.loaded)
            for part, (cs, hs) in enumerate(u.parts):
                wait(eng, unit_done, u.hi_free[part])
                nc.scalar.activation(w_hi[:, u.hi_slot, hs], raw[:, u.slot, cs], ACT.Copy).then_inc(hi_ready, 1)

        def dve_lo(eng, u):
            for part, (cs, hs) in enumerate(u.parts):
                eng.wait_ge(hi_ready, u.ready[part])
                nc.vector.tensor_tensor(w_lo[:, u.slot, cs], raw[:, u.slot, cs],
                                        w_hi[:, u.hi_slot, hs].bitcast(F32), ALU.subtract).then_inc(lo_ready, 1)

        def split_unit(h):
            return Unit(UN[split_units[h]][0])

        def acc_last(group):
            kind, l, *n = group
            return Unit({"in": ("in", l, *n, 1), "uq": ("uq", l, *n), "v": ("ukv", l), "wo": ("wo", l, *n, 1)}[kind])

        H_WO = [split_of[("wo", l, 0, 0)] for l in range(DEPTH)]

        block = ctx.enter_context(nc.Block())

        @block.sync
        def _(sp):
            sp.dma_start(x[:], x_in.rearrange("o (t p) n -> p (o t) n", p=P)).then_inc(x_loaded, 16)
            for n, (name, c, _) in enumerate(UN):
                if name == ("A", 3):
                    sp.wait_ge(acc_dve, 2)
                    sp.dma_start(gate_a[:], b_ada[1:2, 2 * D:3 * D].broadcast_to([P, D])).then_inc(gate_a_row, 16)
                if name == ("wo", 1, 0, 0):
                    sp.wait_ge(ffn_added, 1)
                    sp.dma_start(gate_f[:], b_ada[1:2, 5 * D:6 * D].broadcast_to([P, D])).then_inc(gate_f_row, 16)
                if n >= RAW:
                    sp.wait_ge(unit_done, done_of[n - RAW])
                sp.dma_start(raw[:, n % RAW, 0:c],
                             w_static[offset[n]:offset[n] + P * c].rearrange("(p c) -> p c", p=P)).then_inc(raw_loaded[n % RAW], 16)

            def expert_units(p, expert):
                for r in range(UPP):
                    n = N_STATIC + r
                    if r >= RAW:
                        sp.wait_ge(unit_done, Unit(r - RAW, p).done)
                    elif isinstance(p, int):
                        sp.wait_ge(unit_done, done_of[n - RAW])
                    else:
                        sp.wait_ge(unit_done, p * (2 * UPP) + (done_of[-1] + 2 * (r + 1 - RAW)))
                    sp.dma_start(raw[:, n % RAW, :], w_moe[bass.ds(expert, 1), r].rearrange("e p c -> p (e c)"))\
                        .then_inc(raw_loaded[n % RAW], 16)

            expert_units(0, 0)
            sp.wait_ge(tables, 1)
            n_pass = sp.value_load(pass_i[0:1, MAX_PASS + 1:MAX_PASS + 2], min_val=EXPERTS, max_val=MAX_PASS)
            with sp.Fori(1, n_pass) as p:
                expert = sp.value_load(pass_i[0:1, bass.ds(p, 1)], min_val=0, max_val=EXPERTS - 1)
                expert_units(p, expert)
            sp.wait_ge(acc_dve, 4)
            sp.dma_start(gate_a[:], g_final.unsqueeze(0).broadcast_to([P, D])).then_inc(gate_a_row, 16)
            for t in range(TILES):
                sp.wait_ge(final_ready, t + 1)
                sp.dma_start(out[0, t * P:(t + 1) * P, :], xn[:, t, :]).then_inc(stored, 16)
            sp.wait_ge(stored, 16 * TILES)

        @block.gpsimd
        def _(pool):
            nc.gpsimd.memset(neg_half[:], -0.5).then_inc(pool_step, 1)
            pool.wait_ge(pool_step, 1)
            done = 1
            for (kind, l), r in rms.items():
                parts = {"lat": [(0, 2, Q_RANK), (2, 4, KV_RANK)], "sub": [(0, 8, 2 * QK)]}.get(kind, [(0, 2, D)])
                pool.wait_ge(ssq_ready, r + 1)
                for a, b, width in parts:
                    nc.gpsimd.tensor_scalar(ms[:, r, a:b], ssq[:, r, a:b], 1.0 / width, EPS, ALU.mult, ALU.add).then_inc(pool_step, 1)
                    done += 1
                pool.wait_ge(pool_step, done)
                b = parts[-1][1]
                nc.gpsimd.tensor_tensor(rstd[:, r, 0:b], ms[:, r, 0:b], neg_half[:, 0:b], ALU.pow).then_inc(rstd_ready, 1)

        @block.scalar
        def _(act):
            act.dma_start(cols[:], cols_in).then_inc(small_loaded, 16)
            act.dma_start(consts[:], consts_in).then_inc(small_loaded, 16)
            act.dma_start(pos_i[:], pos_cols).then_inc(small_loaded, 16)
            act.dma_start(posk_i[:], pos_in.broadcast_to([P, SEQ])).then_inc(small_loaded, 16)
            act.dma_start(rb[:].rearrange("p b h -> p (b h)"),
                          rel_bias.rearrange("(o b) h -> o (b h)", o=1).broadcast_to([P, BUCKETS * DIFF_HEADS])).then_inc(small_loaded, 16)
            act.dma_start(lam_rows[:].rearrange("p l a d -> p (l a d)"),
                          diff_lambda.rearrange("(o l) a d -> o (l a d)", o=1).broadcast_to([P, DEPTH * 4 * QK])).then_inc(small_loaded, 16)
            act.dma_start(gate_a[:], b_ada[0:1, 2 * D:3 * D].broadcast_to([P, D])).then_inc(gate_a_row, 16)
            act.dma_start(gate_f[:], b_ada[0:1, 5 * D:6 * D].broadcast_to([P, D])).then_inc(gate_f_row, 16)
            act.wait_ge(small_loaded, 96)
            nc.scalar.activation(cond[:], col("c"), ACT.Silu).then_inc(silu_c, 1)
            act.wait_ge(lam_summed, 4)
            nc.scalar.activation(lam_exp[:], lam_sum[:], ACT.Exp).then_inc(lam_exped, 1)
            act.wait_ge(angles, 1)
            nc.scalar.activation(sin[:], ang[:], ACT.Sin).then_inc(trig, 1)
            nc.scalar.activation(cos[:], ang_c[:], ACT.Sin).then_inc(trig, 1)

            def squares(event, parts):
                for i, (src, dst, c) in enumerate(parts):
                    ins = nc.scalar.activation(dst, src, ACT.Square, accum_out=ssq[:, rms[event], c:c + 1])
                ins.then_inc(ssq_ready, 1)

            def x_squares(event):
                squares(event, [(x[:, t, :], xn[:, t, :], t) for t in range(TILES)])

            def ada_partials(G):
                act.wait_ge(unit_done, Unit(("ada", *ada_groups[G], 1)).done)
                wait(act, ada_comb, G - 1)
                nc.scalar.activation(ada_p[:, G % 2, :], ADA, ACT.Copy).then_inc(ada_part, 1)

            def evac_split(fill, scale, shift):
                f, s = fill_of[fill], sfill_of[fill]
                act.wait_ge(filled, f + 1)
                wait(act, split_t, 2 * (s - 1))
                for i in range(len(scale)):
                    ins = nc.scalar.activation(h32[:, s % 2, i * SEQ:(i + 1) * SEQ], bank[4 + f % 3][:, i * SEQ:(i + 1) * SEQ],
                                               ACT.Identity, bias=shift[i] if shift else 0.0, scale=scale[i])
                ins.then_inc(evacuated, 1)

            def evac_copy(fill, dst, rows=P):
                f = fill_of[fill]
                act.wait_ge(filled, f + 1)
                nc.scalar.activation(dst, bank[4 + f % 3][0:rows, :], ACT.Copy).then_inc(evacuated, 1)

            def evac_h(kind, l):
                k = 2 * l + (kind == "f")
                base = 24 if kind == "f" else 0
                act.wait_ge(mod_ready, k + 1)
                for i in range(4):
                    c = [2 * i, 2 * i + 1]
                    evac_split((kind, l, i), [mod_a[:, k, j:j + 1] for j in c], [mod[:, l, base + j:base + j + 1] for j in c])

            def evac_acc(group, dst0, dst1, width, view=None):
                q = acc_of[group]
                if group[0] == "kn":
                    act.wait_ge(kn_done, group[1] + 1)
                else:
                    act.wait_ge(unit_done, acc_last(group).done)
                for t, dst in ((0, dst0), (1, dst1)):
                    src = bank[2 * (q % 2) + t][:, 0:width]
                    ins = nc.scalar.activation(dst, view(src) if view else src, ACT.Copy)
                ins.then_inc(acc_act, 1)

            def attention(l):
                def copy_pT(s):
                    S = NS * l + s
                    act.wait_ge(pT_filled, S + 1)
                    wait(act, pv_done, S - 1)
                    w = 2 * n_keys(s)
                    nc.scalar.activation(pT[s % 2][:, 0:w], bank[3 + s % 2][:, 0:w], ACT.Copy).then_inc(pT_ready, 1)

                first = 4 if l == 0 else 22
                n_ada = 8 if l == 0 else 2
                for s in range(NS + 1):
                    S = NS * l + s
                    if s >= 2 and s % 2 == 0 and s // 2 <= n_ada:
                        ada_partials(first + s // 2 - 1)
                    if s < NS:
                        act.wait_ge(soft, 2 * (S + 1))
                        n = n_keys(s)
                        for hh in range(2):
                            nc.scalar.activation(probs[:, s % 3, hh, 0:n], probs[:, s % 3, hh, 0:n], ACT.Exp,
                                                 bias=neg_max[:, s, hh:hh + 1], accum_out=psum_p[:, s, hh:hh + 1]).then_inc(exped, 1)
                    if s:
                        copy_pT(s - 1)

            def layer_attention(l):
                h0 = split_of[("in", l, 0, 0)]
                if l == 0:
                    act.wait_ge(x_loaded, 16)
                    x_squares(("h", 0))
                    for G in range(4):
                        ada_partials(G)
                else:
                    act_hi(act, split_unit(h0 + 2))
                    act.wait_ge(ffn_added, 1)
                    x_squares(("h", 1))
                evac_h("h", l)
                if l == 0:
                    for h in range(3):
                        act_hi(act, split_unit(h))
                for gi, (name, _, w) in enumerate(IN_GROUPS):
                    act_hi(act, split_unit(h0 + 2 * gi + 3))
                    dst = {"mq": mq, "mkv": mkv, "dq": dq, "dk": dk, "dv": dv}[name]
                    evac_acc(("in", l, gi), dst[:, 0, :], dst[:, 1, :], w)
                    act_hi(act, split_unit(h0 + 2 * gi + 4))
                    if name == "mkv":
                        act.wait_ge(acc_act, acc_free[acc_of[("in", l, 1)]][1])
                        squares(("lat", l), [(mq[:, t, :], h32[:, t, 0:Q_RANK], t) for t in range(TILES)] +
                                [(mkv[:, t, 0:KV_RANK], ada_p[:, t, 0:KV_RANK], 2 + t) for t in range(TILES)])
                evac_split(("mq", l, 0), [q_gain[:, l, i:i + 1] for i in (0, 1)], None)
                evac_split(("mq", l, 1), [q_gain[:, l, 2:3]], None)
                evac_split(("ckv", l, 0), [kv_gain[:, l, i:i + 1] for i in (0, 1)], None)
                for qk in range(2):
                    for hp in range(2):
                        evac_copy(("dT", l, qk, hp), dT[:, qk, hp, :])
                for u in range(2):
                    evac_acc(("uq", l, u), qfull[:, 0, u * 384:(u + 1) * 384], qfull[:, 1, u * 384:(u + 1) * 384], 384)
                evac_acc(("kn", l), kfull[:, 0, :, 0:QK], kfull[:, 1, :, 0:QK], NB,
                         lambda s: s.rearrange("p (h d) -> p h d", d=QK))
                evac_acc(("v", l), vm[:, 0, :], vm[:, 1, :], NB)
                for qk in range(2):
                    for hp in range(4):
                        evac_copy(("mT", l, qk, hp), mT[0:MD, qk, hp, :], MD)
                attention(l)
                act.wait_ge(o_ready, NS * l + 8)
                squares(("sub", l), [(o[:, t, h * P:(h + 1) * P], h32[:, 0, (4 * t + h) % 4 * P:((4 * t + h) % 4 + 1) * P]
                                      if t == 0 else h32[:, 1, h * P:(h + 1) * P], 4 * t + h)
                                     for t in range(TILES) for h in range(DIFF_HEADS)])
                for i in range(3):
                    act_hi(act, split_unit(H_WO[l] + i))
                for i in range(4):
                    evac_split(("o", l, i), [o_scale[:, l, j:j + 1] for j in (2 * i, 2 * i + 1)], None)
                act_hi(act, split_unit(H_WO[l] + 3))
                for i in range(3 if l == 0 else 0):
                    act_hi(act, split_unit(H_WO[l] + 4 + i))
                if l == 1:
                    for i in range(2):
                        act_hi(act, Unit(i, 0))
                act.wait_ge(acc_dve, 2 * (l + 1))
                x_squares(("f", l))
                evac_h("f", l)

            def silu_part(j, tiles, up, base_s):
                act.wait_ge(unit_done, up.done)
                wait(act, act_done, base_s + tiles * j)
                for t in range(tiles):
                    b = bank[4 + t] if tiles == 2 else bank[2 + j % 2]
                    nc.scalar.activation(silu[:, t, :], b[:, 0:FB], ACT.Silu).then_inc(silu_done, 1)

            def aT_hi_part(j, tiles, base_h):
                act.wait_ge(aT_filled, base_h + (j + 1))
                b = bank[6 if tiles == 2 else 4]
                w = 2 * P * tiles
                nc.scalar.activation(aT[tiles][0][:, j % 2, 0:w], b[:, 0:w], ACT.Copy).then_inc(aT_hi_ready, 1)

            layer_attention(0)
            h0 = split_of[("A", 0)]
            for j in range(BLOCKS):
                act_hi(act, split_unit(h0 + ffn_index[("A", j)] + 3))
                if j:
                    aT_hi_part(j - 1, 2, 0)
                silu_part(j, 2, Unit(("B", j)), 0)
                act_hi(act, split_unit(h0 + ffn_index[("B", j)] + 3))
                if j:
                    act_hi(act, split_unit(h0 + ffn_index[("C", j - 1)] + 3))
                if j < 10:
                    ada_partials(12 + j)
            aT_hi_part(BLOCKS - 1, 2, 0)
            layer_attention(1)

            act.wait_ge(chosen, 1)
            for t in range(TILES):
                nc.scalar.activation(top_w[:, t, 1:2], top_v[:, t, 1:2], ACT.Exp, bias=top_w[:, t, 0:1]).then_inc(top_exp, 1)

            def evac_gathered(base):
                for b in range(2):
                    act.wait_ge(gathered, base * 2 + (b + 1))
                    if b == 0:
                        wait(act, xg_split, base * 2)
                    for c in range(4 * b, 4 * b + 4):
                        ins = nc.scalar.activation(xg32[:, c, :], bank[5 + b][:, (c % 4) * P:(c % 4 + 1) * P], ACT.Identity,
                                                   bias=mod[:, 1, 24 + c:25 + c], scale=mod_a[:, 3, c:c + 1])
                    ins.then_inc(xg_evac, 1)

            evac_gathered(0)
            act.wait_ge(tables, 1)
            n_pass = act.value_load(pass_i[0:1, MAX_PASS + 1:MAX_PASS + 2], min_val=EXPERTS, max_val=MAX_PASS)
            with act.Fori(0, n_pass) as p:
                base_h = p * BLOCKS + BLOCKS
                base_s = p * BLOCKS + 2 * BLOCKS
                act_hi(act, Unit(2, p))
                act.wait_ge(token_filled, p + 1)
                nc.scalar.activation(token_of[:], bank[7][:, 0:SEQ], ACT.Copy).then_inc(token_ready, 1)
                for j in range(BLOCKS):
                    if ffn_index[("A", j)] + 3 < UPP:
                        act_hi(act, Unit(ffn_index[("A", j)] + 3, p))
                    if j:
                        aT_hi_part(j - 1, 1, base_h)
                    silu_part(j, 1, Unit(ffn_index[("B", j)], p), base_s)
                    if ffn_index[("B", j)] + 3 < UPP:
                        act_hi(act, Unit(ffn_index[("B", j)] + 3, p))
                    if j and ffn_index[("C", j - 1)] + 3 < UPP:
                        act_hi(act, Unit(ffn_index[("C", j - 1)] + 3, p))
                    if j == 5:
                        evac_gathered(p + 1)
                aT_hi_part(BLOCKS - 1, 1, base_h)
                with act.If(p + 1 < n_pass):
                    for r in range(2):
                        act_hi(act, Unit(UPP + r, p))
                act.wait_ge(unit_done, Unit(ffn_index[("C", BLOCKS - 1)], p).done)
                for b in range(2):
                    nc.scalar.activation(y_hi[:, b * NB:(b + 1) * NB], bank[b], ACT.Copy).then_inc(y_hi_ready, 1)
            for t in range(TILES):
                act.wait_ge(moe_in_x, t + 1)
                ins = nc.scalar.activation(xn[:, t, :], x[:, t, :], ACT.Square, accum_out=ssq[:, rms[("final", 1)], t:t + 1])
            ins.then_inc(ssq_ready, 1)

        @block.vector
        def _(dve):
            steps_done = [0]

            def link(ins):
                steps_done[0] += 1
                ins.then_inc(dve_step, 1)
                dve.wait_ge(dve_step, steps_done[0])

            def mark(ins):
                steps_done[0] += 1
                ins.then_inc(dve_step, 1)
                return steps_done[0]

            mark(nc.vector.memset(ones[:], 1.0))
            dve.wait_ge(small_loaded, 96)
            dve.wait_ge(silu_c, 1)
            nc.vector.tensor_copy(cond_rep[:], cond[:].unsqueeze(2).to_broadcast([P, KC, 32])).then_inc(cond_ready, 1)
            for l in range(DEPTH):
                for i in range(2):
                    nc.vector.tensor_tensor_reduce(out=rot[:, 2 * l + i, 0:QK], in0=lam_rows[:, l, 2 * i, :], in1=lam_rows[:, l, 2 * i + 1, :],
                                                   scale=1.0, scalar=0.0, op0=ALU.mult, op1=ALU.add,
                                                   accum_out=lam_sum[:, 2 * l + i:2 * l + i + 1]).then_inc(lam_summed, 1)
            link(nc.vector.tensor_copy(posq[:], pos_i[:]))
            for t in range(TILES):
                link(nc.vector.tensor_scalar(ang[:, t, :], const("freq"), posq[:, t:t + 1], None, ALU.mult))
            magic = 1.5 * 2.0 ** 23
            link(nc.vector.tensor_scalar(turns[:], ang[:], 1.0 / (2 * math.pi), magic, ALU.mult, ALU.add))
            link(nc.vector.tensor_scalar(turns[:], turns[:], magic, None, ALU.subtract))
            c1 = 6.28125
            c2 = 0.0019340515136718750
            c3 = 2 * math.pi - c1 - c2
            for c in (c1, c2, c3):
                link(nc.vector.scalar_tensor_tensor(ang[:], turns[:], -c, ang[:], ALU.mult, ALU.add))
            link(nc.vector.tensor_scalar(ang_c[:], ang[:], math.pi / 2, None, ALU.add))
            link(nc.vector.tensor_scalar(turns[:], ang_c[:], math.pi, -2 * math.pi, ALU.is_gt, ALU.mult))
            link(nc.vector.tensor_tensor(ang_c[:], ang_c[:], turns[:], ALU.add))
            lim = 3.1415925
            link(nc.vector.tensor_scalar(ang_c[:], ang_c[:], lim, -lim, ALU.min, ALU.max))
            nc.vector.tensor_scalar(ang[:], ang[:], lim, -lim, ALU.min, ALU.max).then_inc(angles, 1)
            dve.wait_ge(lam_exped, 1)
            for l in range(DEPTH):
                link(nc.vector.tensor_tensor(neg_lam[:, l:l + 1], lam_exp[:, 2 * l + 1:2 * l + 2], lam_exp[:, 2 * l:2 * l + 1], ALU.subtract))
                link(nc.vector.tensor_scalar(neg_lam[:, l:l + 1], neg_lam[:, l:l + 1], LAM_INIT[l], None, ALU.subtract))
                mark(nc.vector.memset(o_scale[:, l, 4:8], 1.0))
                mark(nc.vector.tensor_scalar(o_scale[:, l, 0:4], ones[:, 0:4], col("subln")[:, l:l + 1], 1.0 - LAM_INIT[l], ALU.mult, ALU.mult))

            link(nc.vector.tensor_copy(posk[:], posk_i[:]))
            for t, (a, b) in enumerate(((0, P), (P, 384))):
                link(nc.vector.tensor_scalar(dist[:, a:b], posk[:, 0:b - a], posq[:, t:t + 1], -1.0, ALU.subtract, ALU.mult))
            link(nc.vector.tensor_tensor(rb_step[:], rb[:, 1:BUCKETS, :], rb[:, 0:BUCKETS - 1, :], ALU.subtract))
            last_bias = [mark(nc.vector.tensor_scalar(bias[:, h, :], const("mask"), rb[:, 0, h:h + 1], None, ALU.add))
                         for h in range(DIFF_HEADS)]
            last_far = [0, 0]

            def bias_steps():
                for b in range(BUCKETS - 1):
                    wait(dve, dve_step, last_far[b % 2])
                    link(nc.vector.tensor_scalar(far[:, b % 2, :], dist[:], float(THRESHOLDS[b]), None, ALU.is_ge))
                    for h in range(DIFF_HEADS):
                        dve.wait_ge(dve_step, last_bias[h])
                        last_bias[h] = mark(nc.vector.scalar_tensor_tensor(
                            bias[:, h, :], far[:, b % 2, :], rb_step[:, b, h:h + 1], bias[:, h, :], ALU.mult, ALU.add))
                    last_far[b % 2] = last_bias[-1]
                    yield

            bias_work = bias_steps()

            def bias_more(n):
                for _ in range(n):
                    next(bias_work, None)

            def ada_take(G):
                l, g = ada_groups[G]
                dve.wait_ge(ada_comb, G + 1)
                if g in (4, 5, 10, 11):
                    gate, row = (gate_a, gate_a_row) if g < 6 else (gate_f, gate_f_row)
                    dve.wait_ge(row, 16 * (l + 1))
                    half = gate[:, (g % 2) * NB:(g % 2 + 1) * NB]
                    nc.vector.scalar_tensor_tensor(half, ADA, 1.0, half, ALU.add, ALU.add).then_inc(ada_used, 1)
                else:
                    nc.vector.tensor_tensor(mod[:, l, 4 * g:4 * g + 4], ADA[:, 0:4], b_col[:, l, 4 * g:4 * g + 4], ALU.add).then_inc(ada_used, 1)
                if g in (3, 9):
                    k = 2 * l + (g == 9)
                    dve.wait_ge(ada_used, G + 1)
                    base, gain = (8, g_attn) if g == 3 else (32, g_ffn)
                    nc.vector.scalar_tensor_tensor(mod_a[:, k, :], mod[:, l, base:base + 8], 1.0, gain[:, l, :], ALU.add, ALU.mult).then_inc(mod_ready, 1)

            def normalise_x(event):
                r = rms[event]
                dve.wait_ge(rstd_ready, r + 1)
                for t in range(TILES):
                    ins = nc.vector.tensor_scalar(xn[:, t, :], x[:, t, :], rstd[:, r, t:t + 1], None, ALU.mult)
                ins.then_inc(xn_ready, 1)

            def split_fill(fill, chunk, n):
                f, s = fill_of[fill], sfill_of[fill]
                dve.wait_ge(evacuated, f + 1)
                src = h32[:, s % 2, 0:n * SEQ]
                hi = TH[:, chunk:chunk + n, :].rearrange("p c t -> p (c t)")
                lo = TL[:, chunk:chunk + n, :].rearrange("p c t -> p (c t)")
                nc.vector.tensor_copy(hi, src).then_inc(split_t, 1)
                dve.wait_ge(split_t, 2 * s + 1)
                nc.vector.tensor_tensor(lo, src, hi.bitcast(F32), ALU.subtract).then_inc(split_t, 1)

            def rope(src1, src2, dst1, dst2, shape, first):
                c, s = cos[:], sin[:]
                if len(shape) == 4:
                    c, s = (a.unsqueeze(2).to_broadcast(shape) for a in (c, s))
                n = shape[1] * shape[-1] * (shape[2] if len(shape) == 4 else 1)

                def part(i):
                    v = rot[:, i, 0:n]
                    if len(shape) == 4:
                        return v.rearrange("p (t h i) -> p t h i", t=shape[1], h=shape[2])
                    return v.rearrange("p (t i) -> p t i", t=shape[1])

                for i, (a, b) in enumerate(((src1, c), (src2, s), (src2, c), (src1, s))):
                    last = mark(nc.vector.tensor_tensor(part(i), a, b, ALU.mult))
                dve.wait_ge(dve_step, last)
                mark(nc.vector.tensor_tensor(dst1, part(0), part(1), ALU.subtract))
                return nc.vector.tensor_tensor(dst2, part(2), part(3), ALU.add)

            def attention(l):
                kinds = {}

                def take_o(s):
                    S = NS * l + s
                    kind, hp, t, m = steps[s]
                    b = bank[5 + s % 2]
                    dve.wait_ge(recip, S + 1)
                    if kind == "diff" and m == 1:
                        link(nc.vector.tensor_scalar(rec_lam[:, s, :], rec[:, s, :], neg_lam[:, l:l + 1], None, ALU.mult))
                    dve.wait_ge(pv_done, S + 1)
                    if kind == "mla":
                        dst = o[:, t, NB + hp * P:NB + (hp + 1) * P].rearrange("p (a d) -> p a d", a=2)
                        nc.vector.tensor_tensor(dst, b[:, 0:P].rearrange("p (a d) -> p a d", a=2),
                                                rec[:, s, :].unsqueeze(2).to_broadcast([P, 2, QK]), ALU.mult).then_inc(o_ready, 1)
                    elif m == 0:
                        dst = o[:, t, hp * 2 * P:(hp + 1) * 2 * P].rearrange("p (a d) -> p a d", a=2)
                        nc.vector.tensor_tensor(dst, b[:, 0:2 * P].rearrange("p (a d) -> p a d", a=2),
                                                rec[:, s, :].unsqueeze(2).to_broadcast([P, 2, P]), ALU.mult).then_inc(o_ready, 1)
                    else:
                        dve.wait_ge(o_ready, S)
                        for hh in range(2):
                            dst = o[:, t, (2 * hp + hh) * P:(2 * hp + hh + 1) * P]
                            ins = nc.vector.scalar_tensor_tensor(dst, b[:, hh * P:(hh + 1) * P], rec_lam[:, s, hh:hh + 1], dst, ALU.mult, ALU.add)
                        ins.then_inc(o_ready, 1)

                first = 4 if l == 0 else 22
                n_ada = 8 if l == 0 else 2
                for s in range(NS + 2):
                    S = NS * l + s
                    if s < NS:
                        kind, hp, t, m = steps[s]
                        n = n_keys(s)
                        b = bank[s % 3].rearrange("p (a k) -> p a k", a=2)[:, :, 0:n]
                        at = 0 if t == 0 else P
                        if kind == "diff":
                            add, scale = bias[:, 2 * hp:2 * hp + 2, at:at + n], QK ** -0.5
                        else:
                            add, scale = const("mask")[:, at:at + n].unsqueeze(1).to_broadcast([P, 2, n]), MD ** -0.5
                        dve.wait_ge(scored, S + 1)
                        if s >= 3:
                            dve.wait_ge(pT_filled, S - 2)
                        w = probs[:, s % 3, :, 0:n]
                        nc.vector.scalar_tensor_tensor(w, b, scale, add, ALU.mult, ALU.add).then_inc(soft, 1)
                        dve.wait_ge(soft, 2 * S + 1)
                        nc.vector.tensor_reduce(neg_max[:, s, :], w, AX.X, ALU.max, negate=True).then_inc(soft, 1)
                    if 1 <= s <= NS:
                        dve.wait_ge(exped, 2 * S)
                        nc.vector.reciprocal(rec[:, s - 1, :], psum_p[:, s - 1, :]).then_inc(recip, 1)
                    if s >= 2 and s % 2 == 0 and s // 2 <= n_ada:
                        ada_take(first + s // 2 - 1)
                    if s >= 2:
                        take_o(s - 2)

            def layer_attention(l):
                h0 = split_of[("in", l, 0, 0)]
                if l == 1:
                    dve_lo(dve, split_unit(h0 + 2))
                normalise_x(("h", l))
                if l == 0:
                    for G in range(4):
                        bias_more(2)
                        ada_take(G)
                for i in range(4):
                    split_fill(("h", l, i), 2 * i, 2)
                if l == 0:
                    for h in range(3):
                        dve_lo(dve, split_unit(h))
                for gi in range(5):
                    dve_lo(dve, split_unit(h0 + 2 * gi + 3))
                    bias_more(2)
                    dve_lo(dve, split_unit(h0 + 2 * gi + 4))
                    bias_more(2)
                    if gi == 2:
                        r = rms[("lat", l)]
                        dve.wait_ge(rstd_ready, r + 1)
                        for t in range(TILES):
                            nc.vector.tensor_scalar(mq[:, t, :], mq[:, t, :], rstd[:, r, t:t + 1], None, ALU.mult)
                            ins = nc.vector.tensor_scalar(mkv[:, t, 0:KV_RANK], mkv[:, t, 0:KV_RANK], rstd[:, r, 2 + t:3 + t], None, ALU.mult)
                        ins.then_inc(xn_ready, 1)
                split_fill(("mq", l, 0), 0, 2)
                split_fill(("mq", l, 1), 2, 1)
                split_fill(("ckv", l, 0), 4, 2)
                bias_more(BUCKETS)
                dve.wait_ge(trig, 2)
                dve.wait_ge(split_t, 2 * (sfill_of[("ckv", l, 0)] + 1))
                k1, k2 = mkv[:, :, KV_RANK:KV_RANK + HALF], mkv[:, :, KV_RANK + HALF:MKV]
                link(rope(k1, k2, k1, k2, [P, TILES, HALF], True))
                dve.wait_ge(acc_act, acc_free[acc_of[("v", l)]][1])
                for t in range(TILES):
                    mark(nc.vector.tensor_copy(kfull[:, t, :, QK:MD], mkv[:, t, KV_RANK:MKV].unsqueeze(1).to_broadcast([P, MLA_HEADS, ROPE])))
                q4 = qfull[:].rearrange("p t (h d) -> p t h d", d=MD)
                q1, q2 = q4[:, :, :, QK:QK + HALF], q4[:, :, :, QK + HALF:MD]
                rope(q1, q2, q1, q2, [P, TILES, MLA_HEADS, HALF], False).then_inc(roped, 1)
                attention(l)
                r = rms[("sub", l)]
                dve.wait_ge(rstd_ready, r + 1)
                for t in range(TILES):
                    v = o[:, t, 0:NB].rearrange("p (h d) -> p h d", h=DIFF_HEADS)
                    ins = nc.vector.tensor_tensor(v, v, rstd[:, r, 4 * t:4 * t + 4].unsqueeze(2).to_broadcast([P, DIFF_HEADS, P]), ALU.mult)
                ins.then_inc(xn_ready, 1)
                for i in range(3):
                    dve_lo(dve, split_unit(H_WO[l] + i))
                for i in range(4):
                    split_fill(("o", l, i), 2 * i, 2)
                dve_lo(dve, split_unit(H_WO[l] + 3))
                for nh in range(2):
                    q = acc_of[("wo", l, nh)]
                    if nh == 1:
                        for i in range(2):
                            dve_lo(dve, split_unit(H_WO[l] + 4 + i) if l == 0 else Unit(i, 0))
                    dve.wait_ge(unit_done, acc_last(("wo", l, nh)).done)
                    cs = slice(nh * NB, (nh + 1) * NB)
                    wait(dve, acc_dve, 2 * l + nh)
                    gated_add(gate_a, [(2 * (q % 2) + t, t, cs) for t in range(TILES)]).then_inc(acc_dve, 1)
                if l == 0:
                    dve_lo(dve, split_unit(H_WO[l] + 6))
                normalise_x(("f", l))
                for i in range(4):
                    split_fill(("f", l, i), 2 * i, 2)

            def gated_add(gate, parts):
                scaled, added = [], []
                wait(dve, dve_step, steps_done[0])
                for i in range(len(parts) + 1):
                    if i < len(parts):
                        b, t, cs = parts[i]
                        if i >= 2:
                            dve.wait_ge(dve_step, added[i - 2])
                        scaled.append(mark(nc.vector.tensor_tensor(tmp[:, i % 2, :], bank[b], gate[:, cs], ALU.mult)))
                    if i:
                        b, t, cs = parts[i - 1]
                        dve.wait_ge(dve_step, scaled[i - 1])
                        ins = nc.vector.tensor_tensor(x[:, t, cs], x[:, t, cs], tmp[:, (i - 1) % 2, :], ALU.add)
                        if i < len(parts):
                            added.append(mark(ins))
                return ins

            def act_part(j, tiles, base_s):
                for t in range(tiles):
                    dve.wait_ge(silu_done, base_s + (tiles * j + t + 1))
                    if t == 0:
                        wait(dve, aT_filled, (base_s if isinstance(base_s, int) else base_s - BLOCKS) + j)
                    b = bank[4 + t] if tiles == 2 else bank[2 + j % 2]
                    nc.vector.tensor_tensor(act_f[:, t, :], b[:, FB:2 * FB], silu[:, t, :], ALU.mult).then_inc(act_done, 1)

            def aT_lo_part(j, tiles, base_h):
                dve.wait_ge(aT_hi_ready, base_h + (j + 1))
                b = bank[6 if tiles == 2 else 4]
                w = 2 * P * tiles
                nc.vector.tensor_tensor(aT[tiles][1][:, j % 2, 0:w], b[:, 0:w], aT[tiles][0][:, j % 2, 0:w].bitcast(F32), ALU.subtract).then_inc(aT_lo_ready, 1)

            layer_attention(0)
            h0 = split_of[("A", 0)]
            for j in range(BLOCKS):
                dve_lo(dve, split_unit(h0 + ffn_index[("A", j)] + 3))
                if j:
                    aT_lo_part(j - 1, 2, 0)
                act_part(j, 2, 0)
                dve_lo(dve, split_unit(h0 + ffn_index[("B", j)] + 3))
                if j:
                    dve_lo(dve, split_unit(h0 + ffn_index[("C", j - 1)] + 3))
                if j < 10:
                    ada_take(12 + j)
            aT_lo_part(BLOCKS - 1, 2, 0)
            dve.wait_ge(unit_done, Unit(("C", BLOCKS - 1)).done)
            gated_add(gate_f, [(b, b // 2, slice((b % 2) * NB, (b % 2 + 1) * NB)) for b in range(4)]).then_inc(ffn_added, 1)
            layer_attention(1)

            dve.wait_ge(xn_ready, 8)
            xn2 = xn[:].rearrange("p t n -> p (t n)")
            hi2, lo2 = (a[:].rearrange("p t n -> p (t n)") for a in (xn_hi, xn_lo))
            link(nc.vector.tensor_copy(hi2, xn2))
            link(nc.vector.tensor_tensor(lo2, xn2, hi2.bitcast(F32), ALU.subtract))
            link(nc.vector.tensor_copy(router_hi[:], col("router")))
            nc.vector.tensor_tensor(router_lo[:], col("router"), router_hi[:].bitcast(F32), ALU.subtract).then_inc(xn_split, 1)
            dve.wait_ge(routed, 1)
            link(nc.vector.tensor_copy(rl[:].rearrange("p t e -> p (t e)"), bank[7][:, 0:TILES * EXPERTS]))
            for t in range(TILES):
                link(nc.vector.max(top_v[:, t, :], rl[:, t, :]))
                link(nc.vector.max_index(top_i[:, t, :], top_v[:, t, :], rl[:, t, :]))
            link(nc.vector.tensor_copy(top_f[:], top_i[:]))
            nc.vector.tensor_scalar(top_w[:, :, 0:1], top_v[:, :, 0:1], -1.0, None, ALU.mult).then_inc(chosen, 1)
            for t in range(TILES):
                for i in range(2):
                    mark(nc.vector.tensor_scalar(hot[:, t, i, :], iota[:, 0:EXPERTS], top_f[:, t, i:i + 1], None, ALU.is_equal))
            link(nc.vector.memset(sel_t[:], 0.0))
            link(nc.vector.tensor_tensor(sel_t[:, :, 0:EXPERTS], hot[:, :, 0, :], hot[:, :, 1, :], ALU.add))
            nc.vector.memset(pos_t[:], 0.0).then_inc(chosen, 1)
            link(nc.vector.memset(gate_t[:], 0.0))
            dve.wait_ge(top_exp, 2)
            link(nc.vector.tensor_scalar(top_w[:, :, 2:3], top_w[:, :, 1:2], 1.0, None, ALU.add))
            link(nc.vector.reciprocal(top_w[:, :, 2:3], top_w[:, :, 2:3]))
            link(nc.vector.tensor_tensor(top_w[:, :, 3:4], top_w[:, :, 1:2], top_w[:, :, 2:3], ALU.mult))
            for t in range(TILES):
                link(nc.vector.tensor_scalar(gate_t[:, t, 0:EXPERTS], hot[:, t, 0, :], top_w[:, t, 2:3], None, ALU.mult))
                link(nc.vector.scalar_tensor_tensor(gate_t[:, t, 0:EXPERTS], hot[:, t, 1, :], top_w[:, t, 3:4], gate_t[:, t, 0:EXPERTS], ALU.mult, ALU.add))
            dve.wait_ge(placed_ps, 1)
            link(nc.vector.tensor_copy(pos_t[:, :, 0:EXPERTS], bank[7][:, 0:16].rearrange("p (t e) -> p t e", t=TILES)))
            link(nc.vector.tensor_copy(count[:], bank[7][:, 16:24]))

            def build_slots(p):
                for t in range(TILES):
                    ins = nc.vector.tensor_scalar(slot_of[:, t, :], iota, pos_t[:, t, bass.ds(p, 1)], sel_t[:, t, bass.ds(p, 1)],
                                                  ALU.is_equal, ALU.mult)
                ins.then_inc(slots_built, 1)

            build_slots(0)
            mark(nc.vector.memset(rank[:, 0:1], 0.0))
            link(nc.vector.tensor_scalar(over[:], count[:], float(SLOTS), None, ALU.is_gt))
            for e in range(EXPERTS):
                link(nc.vector.tensor_tensor(rank[:, e + 1:e + 2], rank[:, e:e + 1], over[:, e:e + 1], ALU.add))
            link(nc.vector.memset(pass_f[:], 0.0))
            mark(nc.vector.tensor_copy(pass_f[:, 0:EXPERTS], iota[:, 0:EXPERTS]))
            mark(nc.vector.tensor_scalar(pass_f[:, MAX_PASS + 1:MAX_PASS + 2], rank[:, EXPERTS:EXPERTS + 1], float(EXPERTS), None, ALU.add))
            for i in range(MAX_OVER):
                c = EXPERTS + i
                link(nc.vector.scalar_tensor_tensor(over_hot[:, i, :], rank[:, 0:EXPERTS], float(i), over[:], ALU.is_equal, ALU.mult))

                def pick(dst, src):
                    link(nc.vector.tensor_tensor_reduce(out=junk8[:], in0=over_hot[:, i, :], in1=src, scale=1.0, scalar=0.0,
                                                        op0=ALU.mult, op1=ALU.add, accum_out=dst))

                pick(pass_f[:, c:c + 1], iota[:, 0:EXPERTS])
                for t in range(TILES):
                    pick(sel_t[:, t, c:c + 1], sel_t[:, t, 0:EXPERTS])
                    pick(gate_t[:, t, c:c + 1], gate_t[:, t, 0:EXPERTS])
                    pick(pos_t[:, t, c:c + 1], pos_t[:, t, 0:EXPERTS])
            link(nc.vector.tensor_scalar(pos_t[:, :, EXPERTS:MAX_PASS], pos_t[:, :, EXPERTS:MAX_PASS], float(SLOTS), None, ALU.subtract))
            link(nc.vector.memset(moe_out[:], 0.0))
            nc.vector.tensor_copy(pass_i[:], pass_f[:]).then_inc(tables, 1)

            def split_gathered(base):
                dve.wait_ge(xg_evac, base * 2 + 2)
                nc.vector.tensor_copy(xg_hi[:], xg32[:]).then_inc(xg_split, 1)
                dve.wait_ge(xg_split, base * 2 + 1)
                nc.vector.tensor_tensor(xg_lo[:], xg32[:], xg_hi[:].bitcast(F32), ALU.subtract).then_inc(xg_split, 1)

            split_gathered(0)
            dve.wait_ge(tables, 1)
            n_pass = dve.value_load(pass_i[0:1, MAX_PASS + 1:MAX_PASS + 2], min_val=EXPERTS, max_val=MAX_PASS)
            with dve.Fori(0, n_pass) as p:
                base_h = p * BLOCKS + BLOCKS
                base_s = p * BLOCKS + 2 * BLOCKS
                dve_lo(dve, Unit(2, p))
                for j in range(BLOCKS):
                    if ffn_index[("A", j)] + 3 < UPP:
                        dve_lo(dve, Unit(ffn_index[("A", j)] + 3, p))
                    if j:
                        aT_lo_part(j - 1, 1, base_h)
                    act_part(j, 1, base_s)
                    if ffn_index[("B", j)] + 3 < UPP:
                        dve_lo(dve, Unit(ffn_index[("B", j)] + 3, p))
                    if j and ffn_index[("C", j - 1)] + 3 < UPP:
                        dve_lo(dve, Unit(ffn_index[("C", j - 1)] + 3, p))
                    if j == 2:
                        dve.wait_ge(token_filled, p + 1)
                        build_slots(p + 1)
                aT_lo_part(BLOCKS - 1, 1, base_h)
                split_gathered(p + 1)
                with dve.If(p + 1 < n_pass):
                    for r in range(2):
                        dve_lo(dve, Unit(UPP + r, p))
                for b in range(2):
                    dve.wait_ge(y_hi_ready, p * 2 + (b + 1))
                    cs = slice(b * NB, (b + 1) * NB)
                    nc.vector.tensor_tensor(y_lo[:, cs], bank[b], y_hi[:, cs].bitcast(F32), ALU.subtract).then_inc(y_lo_ready, 1)
                for i in range(4):
                    t, cs = i // 2, slice((i % 2) * NB, (i % 2 + 1) * NB)
                    dve.wait_ge(scattered, p * 4 + (i + 1))
                    nc.vector.scalar_tensor_tensor(moe_out[:, t, cs], bank[4 + i], gate_t[:, t, bass.ds(p, 1)], moe_out[:, t, cs],
                                                   ALU.mult, ALU.add).then_inc(moe_added, 1)
            dve.wait_ge(moe_added, n_pass * 4)
            for t in range(TILES):
                link(nc.vector.tensor_tensor(moe_out[:, t, :], moe_out[:, t, :], gate_f[:], ALU.mult))
                nc.vector.tensor_tensor(x[:, t, :], x[:, t, :], moe_out[:, t, :], ALU.add).then_inc(moe_in_x, 1)
            r = rms[("final", 1)]
            dve.wait_ge(rstd_ready, r + 1)
            dve.wait_ge(gate_a_row, 48)
            for t in range(TILES):
                nc.vector.scalar_tensor_tensor(xn[:, t, :], x[:, t, :], rstd[:, r, t:t + 1], gate_a[:], ALU.mult, ALU.mult).then_inc(final_ready, 1)

        @block.tensor
        def _(pe):
            def products(dst, first, last, hi, lo, u, cs):
                wh, wl = w_hi[:, u.hi_slot, u.hi_cols(cs)], w_lo[:, u.slot, cs]
                nc.tensor.matmul(dst, hi, wh, start=first, stop=False)
                nc.tensor.matmul(dst, hi, wl, start=False, stop=False)
                return nc.tensor.matmul(dst, lo, wh, start=False, stop=last)

            def chunk(c, t):
                ts = slice(t * P, (t + 1) * P)
                return TH[:, c, ts], TL[:, c, ts]

            def ada_unit(G, kh):
                l, g = ada_groups[G]
                u = Unit(("ada", l, g, kh))
                pe.wait_ge(raw_loaded[u.slot], u.loaded)
                if kh == 0:
                    wait(pe, ada_used, G)
                for k in range(4):
                    ins = nc.tensor.matmul(ADA[32 * k:32 * k + 32, :], cond_rep[:, 4 * kh + k, :], raw[:, u.slot, k * NB:(k + 1) * NB],
                                           start=(kh == 0), stop=(kh == 1), tile_position=(0, 32 * k))
                ins.then_inc(unit_done, 1)

            def ada_combine(G):
                l, g = ada_groups[G]
                pe.wait_ge(ada_part, G + 1)
                if g in (4, 5, 10, 11):
                    ins = nc.tensor.matmul(ADA, const("selrow"), ada_p[:, G % 2, :], start=True, stop=True)
                else:
                    for c in range(4):
                        ins = nc.tensor.matmul(ADA[:, c:c + 1], ada_p[:, G % 2, c * P:(c + 1) * P], const("selrow")[:, 0:1], start=True, stop=True)
                ins.then_inc(ada_comb, 1)

            def fill(name, blocks, need=None):
                f = fill_of[name]
                wait(pe, evacuated, f - 2)
                for i, (src, rows) in enumerate(blocks):
                    ins = nc.tensor.transpose(bank[4 + f % 3][0:rows, i * P:(i + 1) * P], src, ident)
                ins.then_inc(filled, 1)

            def fill_tokens(kind, l, src, chunks):
                for i in range((chunks + 1) // 2):
                    cs = [c for c in (2 * i, 2 * i + 1) if c < chunks]
                    fill((kind, l, i), [(src(t, c), P) for c in cs for t in range(TILES)])

            def run_group(group, units, chunks_of, width):
                q = acc_of[group]
                if q >= 2:
                    s, v = acc_free[q - 2]
                    pe.wait_ge(s, v)
                for i, u in enumerate(units):
                    cks = chunks_of[i]
                    for k, c in enumerate(cks):
                        if k in (0, 2):
                            pe.wait_ge(lo_ready, u.ready[k // 2])
                        for t in range(TILES):
                            hi, lo = chunk(c, t)
                            ins = products(bank[2 * (q % 2) + t][:, 0:width], i == 0 and k == 0, i == len(units) - 1 and k == len(cks) - 1,
                                           hi, lo, u, slice(k * width, (k + 1) * width))
                        if k in (1, len(cks) - 1):
                            ins.then_inc(unit_done, 1)

            def attention(l):
                def score(s):
                    S = NS * l + s
                    kind, hp, t, m = steps[s]
                    n = n_keys(s)
                    if s >= 3:
                        pe.wait_ge(soft, 2 * (S - 3) + 1)
                    for hh in range(2):
                        dst = bank[s % 3][:, hh * SEQ:hh * SEQ + n]
                        if kind == "diff":
                            rows = slice(QK * m, QK * (m + 1))
                            q_, k_ = dT[rows, 0, hp, :], dT[rows, 1, hp, :]
                        else:
                            q_, k_ = mT[0:MD, 0, hp, :], mT[0:MD, 1, hp, :]
                        ins = nc.tensor.matmul(dst, q_[:, hh * SEQ + t * P:hh * SEQ + (t + 1) * P], k_[:, hh * SEQ:hh * SEQ + n],
                                               start=True, stop=True)
                    ins.then_inc(scored, 1)

                def transpose_probs(s):
                    S = NS * l + s
                    pe.wait_ge(exped, 2 * (S + 1))
                    if s >= 2:
                        pe.wait_ge(pT_ready, S - 1)
                    kb = n_keys(s) // P
                    for hh in range(2):
                        for k in range(kb):
                            i = hh * kb + k
                            ins = nc.tensor.transpose(bank[3 + s % 2][:, i * P:(i + 1) * P], probs[:, s % 3, hh, k * P:(k + 1) * P], ident)
                    ins.then_inc(pT_filled, 1)

                def values(s):
                    S = NS * l + s
                    kind, hp, t, m = steps[s]
                    pe.wait_ge(pT_ready, S + 1)
                    if s >= 2:
                        pe.wait_ge(o_ready, S - 1)
                    kb = n_keys(s) // P
                    dvw = P if kind == "diff" else QK
                    v = dv if kind == "diff" else vm
                    for hh in range(2):
                        h = 2 * hp + hh
                        for k in range(kb):
                            i = hh * kb + k
                            ins = nc.tensor.matmul(bank[5 + s % 2][:, hh * dvw:(hh + 1) * dvw], pT[s % 2][:, i * P:(i + 1) * P],
                                                   v[:, k, h * dvw:(h + 1) * dvw], start=(k == 0), stop=(k == kb - 1))
                    ins.then_inc(pv_done, 1)

                first = 4 if l == 0 else 22
                n_ada = 8 if l == 0 else 2
                pe.wait_ge(acc_act, acc_free[acc_of[("v", l)]][1])
                pe.wait_ge(evacuated, fill_of[("mT", l, 1, 3)] + 1)
                for s in range(NS + 2):
                    if s < NS:
                        score(s)
                    if s >= 2 and s % 2 == 0 and s // 2 <= n_ada:
                        ada_combine(first + s // 2 - 1)
                    if 1 <= s <= NS:
                        transpose_probs(s - 1)
                    if s >= 2:
                        values(s - 2)
                    if s < 2 * n_ada:
                        G = first + s // 2
                        ada_unit(G, s % 2)

            def layer_attention(l):
                pe.wait_ge(xn_ready, rms[("h", l)] + 1)
                fill_tokens("h", l, lambda t, c: xn[:, t, c * P:(c + 1) * P], KC)
                pe.wait_ge(split_t, 2 * (sfill_of[("h", l, 3)] + 1))
                for gi, (_, _, w) in enumerate(IN_GROUPS):
                    run_group(("in", l, gi), [Unit(("in", l, gi, kh)) for kh in range(2)], [range(4), range(4, 8)], w)
                pe.wait_ge(xn_ready, rms[("lat", l)] + 1)
                fill_tokens("mq", l, lambda t, c: mq[:, t, c * P:(c + 1) * P], 3)
                fill_tokens("ckv", l, lambda t, c: mkv[:, t, c * P:(c + 1) * P], 2)
                pe.wait_ge(acc_act, acc_free[acc_of[("in", l, 4)]][1])
                for qk, src in ((0, dq), (1, dk)):
                    for hp in range(2):
                        fill(("dT", l, qk, hp), [(src[:, t, (2 * hp + hh) * P:(2 * hp + hh + 1) * P], P) for hh in range(2) for t in range(TILES)])
                pe.wait_ge(split_t, 2 * (sfill_of[("ckv", l, 0)] + 1))
                for u in range(2):
                    run_group(("uq", l, u), [Unit(("uq", l, u))], [range(3)], 384)
                u = Unit(("ukv", l))
                for n, name in enumerate(("kn", "v")):
                    q = acc_of[(name, l)]
                    pe.wait_ge(*acc_free[q - 2])
                    for k in range(2):
                        pe.wait_ge(lo_ready, u.ready[k])
                        for t in range(TILES):
                            hi, lo = chunk(4 + k, t)
                            off = k * D + n * NB
                            ins = products(bank[2 * (q % 2) + t], k == 0, k == 1, hi, lo, u, slice(off, off + NB))
                        if n == 1:
                            ins.then_inc(unit_done, 1)
                    if n == 0:
                        ins.then_inc(kn_done, 1)
                pe.wait_ge(roped, l + 1)
                for qk in range(2):
                    for hp in range(4):
                        def src(t, h):
                            return qfull[:, t, h * MD:(h + 1) * MD] if qk == 0 else kfull[:, t, h, :]
                        fill(("mT", l, qk, hp), [(src(t, 2 * hp + hh), MD) for hh in range(2) for t in range(TILES)])
                attention(l)
                pe.wait_ge(o_ready, NS * (l + 1))
                pe.wait_ge(xn_ready, rms[("sub", l)] + 1)
                fill_tokens("o", l, lambda t, c: o[:, t, c * P:(c + 1) * P], KC)
                pe.wait_ge(split_t, 2 * (sfill_of[("o", l, 3)] + 1))
                for nh in range(2):
                    run_group(("wo", l, nh), [Unit(("wo", l, nh, kh)) for kh in range(2)], [range(4), range(4, 8)], NB)
                pe.wait_ge(xn_ready, rms[("f", l)] + 1)
                fill_tokens("f", l, lambda t, c: xn[:, t, c * P:(c + 1) * P], KC)
                pe.wait_ge(split_t, 2 * (sfill_of[("f", l, 3)] + 1))

            def up_half(j, kh, tiles, u, stationary, base_s):
                if kh == 0:
                    wait(pe, act_done, base_s + (2 * j if tiles == 2 else j - 1))
                for k in range(4):
                    if k in (0, 2):
                        pe.wait_ge(lo_ready, u.ready[k // 2])
                    for t in range(tiles):
                        hi, lo = stationary(4 * kh + k, t)
                        b = bank[4 + t] if tiles == 2 else bank[2 + j % 2]
                        ins = products(b, kh == 0 and k == 0, kh == 1 and k == 3, hi, lo, u, slice(k * NB, (k + 1) * NB))
                    if k in (1, 3):
                        ins.then_inc(unit_done, 1)

            def transpose_act(j, tiles, base_s, base_h):
                pe.wait_ge(act_done, base_s + tiles * (j + 1))
                wait(pe, aT_lo_ready, base_h + j)
                b = bank[6 if tiles == 2 else 4]
                for c in range(2):
                    for t in range(tiles):
                        i = c * tiles + t
                        ins = nc.tensor.transpose(b[:, i * P:(i + 1) * P], act_f[:, t, c * P:(c + 1) * P], ident)
                ins.then_inc(aT_filled, 1)

            def down(j, tiles, u, base_h):
                pe.wait_ge(aT_lo_ready, base_h + (j + 1))
                for c in range(2):
                    pe.wait_ge(lo_ready, u.ready[c])
                    for t in range(tiles):
                        i = c * tiles + t
                        hi, lo = aT[tiles][0][:, j % 2, i * P:(i + 1) * P], aT[tiles][1][:, j % 2, i * P:(i + 1) * P]
                        for half in range(2):
                            ins = products(bank[2 * t + half], j == 0 and c == 0, j == BLOCKS - 1 and c == 1, hi, lo, u,
                                           slice(c * D + half * NB, c * D + (half + 1) * NB))
                    ins.then_inc(unit_done, 1)

            pe.wait_ge(cond_ready, 1)
            for G in range(4):
                for kh in range(2):
                    ada_unit(G, kh)
                ada_combine(G)
            layer_attention(0)
            pe.wait_ge(acc_dve, 2)
            for j in range(BLOCKS):
                up_half(j, 0, 2, Unit(("A", j)), chunk, 0)
                if j:
                    transpose_act(j - 1, 2, 0, 0)
                up_half(j, 1, 2, Unit(("B", j)), chunk, 0)
                if j:
                    down(j - 1, 2, Unit(("C", j - 1)), 0)
                if j < 10:
                    for kh in range(2):
                        ada_unit(12 + j, kh)
                    ada_combine(12 + j)
            transpose_act(BLOCKS - 1, 2, 0, 0)
            down(BLOCKS - 1, 2, Unit(("C", BLOCKS - 1)), 0)
            pe.wait_ge(ffn_added, 1)
            layer_attention(1)

            pe.wait_ge(xn_split, 1)
            for t in range(TILES):
                for c in range(KC):
                    hi, lo = chunk(c, t)
                    rh, rlo = router_hi[:, c * EXPERTS:(c + 1) * EXPERTS], router_lo[:, c * EXPERTS:(c + 1) * EXPERTS]
                    dst = bank[7][:, t * EXPERTS:(t + 1) * EXPERTS]
                    nc.tensor.matmul(dst, hi, rh, start=(c == 0), stop=False)
                    nc.tensor.matmul(dst, hi, rlo, start=False, stop=False)
                    ins = nc.tensor.matmul(dst, lo, rh, start=False, stop=(c == KC - 1))
            ins.then_inc(routed, 1)
            pe.wait_ge(chosen, 2)
            sel = [sel_t[:, t, 0:EXPERTS] for t in range(TILES)]
            nc.tensor.matmul(bank[7][:, 0:8], const("before"), sel[0], start=True, stop=True)
            nc.tensor.matmul(bank[7][:, 8:16], const("before"), sel[1], start=True, stop=False)
            nc.tensor.matmul(bank[7][:, 8:16], ones[:], sel[0], start=False, stop=True)
            nc.tensor.matmul(bank[7][:, 16:24], ones[:], sel[0], start=True, stop=False)
            nc.tensor.matmul(bank[7][:, 16:24], ones[:], sel[1], start=False, stop=True).then_inc(placed_ps, 1)

            def gather(base):
                pe.wait_ge(slots_built, base + 1)
                for b in range(2):
                    for c in range(4 * b, 4 * b + 4):
                        dst = bank[5 + b][:, (c % 4) * P:(c % 4 + 1) * P]
                        n = 0
                        for t in range(TILES):
                            for part in (xn_hi, xn_lo):
                                ins = nc.tensor.matmul(dst, part[:, t, c * P:(c + 1) * P], slot_of[:, t, :], start=(n == 0), stop=(n == 3))
                                n += 1
                    ins.then_inc(gathered, 1)

            def slots_chunk(c, t):
                return xg_hi[:, c, :], xg_lo[:, c, :]

            gather(0)
            pe.wait_ge(tables, 1)
            n_pass = pe.value_load(pass_i[0:1, MAX_PASS + 1:MAX_PASS + 2], min_val=EXPERTS, max_val=MAX_PASS)
            with pe.Fori(0, n_pass) as p:
                base_h = p * BLOCKS + BLOCKS
                base_s = p * BLOCKS + 2 * BLOCKS
                pe.wait_ge(slots_built, p + 1)
                for t in range(TILES):
                    ins = nc.tensor.transpose(bank[7][:, t * P:(t + 1) * P], slot_of[:, t, :].bitcast(F32), ident)
                ins.then_inc(token_filled, 1)
                pe.wait_ge(xg_split, p * 2 + 2)
                for j in range(BLOCKS):
                    up_half(j, 0, 1, Unit(ffn_index[("A", j)], p), slots_chunk, base_s)
                    if j:
                        transpose_act(j - 1, 1, base_s, base_h)
                    up_half(j, 1, 1, Unit(ffn_index[("B", j)], p), slots_chunk, base_s)
                    if j:
                        down(j - 1, 1, Unit(ffn_index[("C", j - 1)], p), base_h)
                    if j == 5:
                        gather(p + 1)
                transpose_act(BLOCKS - 1, 1, base_s, base_h)
                last = Unit(ffn_index[("C", BLOCKS - 1)], p)
                down(BLOCKS - 1, 1, last, base_h)
                pe.wait_ge(y_lo_ready, p * 2 + 2)
                pe.wait_ge(xg_evac, p * 2 + 4)
                pe.wait_ge(token_ready, p + 1)
                for i in range(4):
                    t, cs = i // 2, slice((i % 2) * NB, (i % 2 + 1) * NB)
                    nc.tensor.matmul(bank[4 + i], token_of[:, t * P:(t + 1) * P], y_hi[:, cs], start=True, stop=False)
                    nc.tensor.matmul(bank[4 + i], token_of[:, t * P:(t + 1) * P], y_lo[:, cs], start=False, stop=True).then_inc(scattered, 1)
                pe.wait_ge(moe_added, p * 4 + 4)


def _chunks(w, width):
    k, n = w.shape
    return w.reshape(k // P, P, n).transpose(1, 0, 2).reshape(P, -1)


def _ffn_units(w1, w3, w2, np):
    out = []
    for kind, j in ffn_order():
        if kind == "C":
            out.append(_chunks(w2[j * FB:(j + 1) * FB], D))
        else:
            rows = slice(0, D // 2) if kind == "A" else slice(D // 2, D)
            cs = slice(j * FB, (j + 1) * FB)
            out.append(_chunks(np.concatenate([w1[rows, cs], w3[rows, cs]], axis=1), NB))
    return out


def _pack(inputs, np):
    f = {k: np.ascontiguousarray(v) for k, v in inputs.items()}
    ffn = dict(zip(ffn_order(), _ffn_units(f["ffn_w1"][0], f["ffn_w3"][0], f["ffn_w2"][0], np)))
    ukv_order = np.arange(MLA_HEADS * 2 * QK).reshape(MLA_HEADS, 2, QK).transpose(1, 0, 2).reshape(-1)
    parts = []
    for name, _, _ in static_units():
        kind = name[0]
        if kind == "ada":
            _, l, g, kh = name
            w = _chunks(f["w_ada"][l][kh * 512:(kh + 1) * 512, g * NB:(g + 1) * NB], NB)
        elif kind == "in":
            _, l, gi, kh = name
            _, c0, width = IN_GROUPS[gi]
            w = _chunks(f["w_in"][l][kh * 512:(kh + 1) * 512, c0:c0 + width], width)
        elif kind == "uq":
            _, l, u = name
            w = _chunks(f["w_uq"][l][:, u * 384:(u + 1) * 384], 384)
        elif kind == "ukv":
            w = _chunks(f["w_ukv"][name[1]][:, ukv_order], D)
        elif kind == "wo":
            _, l, nh, kh = name
            w = _chunks(f["w_o"][l][kh * 512:(kh + 1) * 512, nh * NB:(nh + 1) * NB], NB)
        else:
            w = ffn[name]
        parts.append(w.reshape(-1))
    w_static = np.concatenate(parts)
    w_moe = np.stack([np.stack(_ffn_units(f["moe_w1"][0, e], f["moe_w3"][0, e], f["moe_w2"][0, e], np)) for e in range(EXPERTS)])

    def columns(v):
        return v.reshape(-1, P).T

    cols = np.concatenate([columns(f["g_attn"]), columns(f["g_ffn"]), columns(f["b_ada"]), columns(f["mla_q_norm"]),
                           columns(f["mla_kv_norm"]), columns(f["diff_subln_g"]), columns(f["c"]),
                           _chunks(f["moe_router"][0], EXPERTS)], axis=1)
    r = np.arange(P)
    causal = np.where(r[:, None] >= r[None, :], 0.0, MASKED)
    freq = np.power(np.float32(THETA), -np.arange(HALF, dtype=np.float32) / np.float32(HALF))
    consts = np.concatenate([
        np.eye(P), causal, np.zeros((P, P)), causal,
        r[:, None] < r[None, :],
        np.repeat((r % 32 == 0)[:, None], P, axis=1),
        np.repeat(r[None, :], P, axis=0),
        np.repeat(freq[None, :], P, axis=0)], axis=1).astype(np.float32)
    return {
        "x": f["x"], "positions": f["positions"], "pos_cols": np.ascontiguousarray(columns(f["positions"])),
        "consts": consts, "cols": np.ascontiguousarray(cols),
        "b_ada": f["b_ada"], "rel_bias": f["rel_bias"], "diff_lambda": f["diff_lambda"], "g_final": f["g_final"],
        "w_static": w_static, "w_moe": w_moe,
    }


def kernel(**inputs):
    import numpy as _np
    import concourse.bacc as _bacc
    from concourse import mybir as _mybir
    from concourse.bass_utils import run_bass_kernel_spmd as _run

    nc = _bacc.Bacc("TRN2", target_bir_lowering=False, num_devices=1, dynamic_dma_scratch_size=1024)
    arrays, args = {}, []
    for name, a in _pack({k: _np.asarray(v) for k, v in inputs.items()}, _np).items():
        arrays[f"in_{name}"] = a
        args.append(nc.dram_tensor(f"in_{name}", a.shape, _mybir.dt.from_np(a.dtype), kind="ExternalInput").ap())
    out = nc.dram_tensor("out", (1, SEQ, D), F32, kind="ExternalOutput").ap()
    build(nc, *args, out)
    return _run(nc, [arrays], core_ids=[0]).results[0]["out"]
```

```python
import math
from contextlib import ExitStack

import concourse.bass as bass
from concourse import mybir

F32 = mybir.dt.float32
F32R = mybir.dt.float32r
BF16 = mybir.dt.bfloat16
I32 = mybir.dt.int32
U32 = mybir.dt.uint32
ALU = mybir.AluOpType
ACT = mybir.ActivationFunctionType
AX = mybir.AxisListType

P = 128
D = 1024
SEQ = 256
TILES = SEQ // P
KC = D // P
DEPTH = 2
DIFF_HEADS = 4
MLA_HEADS = 8
QK = 64
ROPE = 32
HALF = ROPE // 2
MD = QK + ROPE
Q_RANK = 384
KV_RANK = 256
MKV = KV_RANK + ROPE
BUCKETS = 32
D_FF = 2816
FB = 256
BLOCKS = D_FF // FB
EXPERTS = 8
SLOTS = P
MAX_OVER = (2 * SEQ) // (SLOTS + 1)
MAX_PASS = EXPERTS + MAX_OVER
EPS = 1e-6
MASKED = -1e30
NB = 512
UNIT = 2048
RAW = 11
HIS = 3
THETA = 10000.0
BIAS_AT = (2, 3, 3, 2, 1)
BIAS_AT_UNIT = 1
BIAS_IN_STEP = 1
BIAS_SPLIT = 21
LAM_INIT = [0.8 - 0.6 * math.exp(-0.3 * l) for l in range(DEPTH)]
THRESHOLDS = list(range(1, 17)) + [math.ceil(16 * 8 ** ((b - 16) / 16) - 1e-9) for b in range(17, BUCKETS)]

IN_GROUPS = [("mq", 1536, Q_RANK), ("mkv", 1920, MKV), ("dq", 0, 512), ("dk", 512, 512), ("dv", 1024, 512)]


def static_units():
    units = []

    def ada(l, g):
        units.extend((("ada", l, g, kh), UNIT, False) for kh in range(2))

    for l in range(DEPTH):
        if l == 0:
            for g in range(4):
                ada(0, g)
        for gi, (_, _, w) in enumerate(IN_GROUPS):
            units.extend((("in", l, gi, kh), 4 * w, True) for kh in range(2))
        units.extend((("uq", l, u), 3 * 384, True) for u in range(2))
        units.append((("ukv", l), UNIT, True))
        for g in (range(4, 12) if l == 0 else range(10, 12)):
            ada(l, g)
        units.extend((("wo", l, nh, kh), UNIT, True) for nh in range(2) for kh in range(2))
        if l == 0:
            for j in range(BLOCKS):
                units.append((("A", j), UNIT, True))
                units.append((("B", j), UNIT, True))
                if j:
                    units.append((("C", j - 1), UNIT, True))
                if j < 10:
                    ada(1, j)
            units.append((("C", BLOCKS - 1), UNIT, True))
    return units


def ffn_order():
    out = []
    for j in range(BLOCKS):
        out += [("A", j), ("B", j)] + ([("C", j - 1)] if j else [])
    return out + [("C", BLOCKS - 1)]


CONSTS = {}
_at = 0
for _n, _w in (("ident", 128), ("mask", 384), ("before", 128), ("selrow", 128), ("iota", 128), ("freq", HALF)):
    CONSTS[_n] = (_at, _at + _w)
    _at += _w
N_CONST = _at
COLS = {}
_at = 0
for _n, _w in (("g_attn", 16), ("g_ffn", 16), ("b_ada", 96), ("q_norm", 6), ("kv_norm", 4), ("subln", 2), ("c", 8),
               ("router", 64)):
    COLS[_n] = (_at, _at + _w)
    _at += _w
N_COLS = _at


def build(nc, x_in, pos_in, pos_cols, consts_in, cols_in, b_ada, rel_bias, diff_lambda, g_final, w_static, w_moe, out):
    UN = static_units()
    N_STATIC = len(UN)
    unit_of = {name: n for n, (name, _, _) in enumerate(UN)}
    offset, at = [], 0
    for _, cols, _ in UN:
        offset.append(at)
        at += P * cols
    split_units = [n for n, u in enumerate(UN) if u[2]]
    split_of = {UN[n][0]: h for h, n in enumerate(split_units)}
    N_SPLIT = len(split_units)
    done_of, at = [], 0
    for _, _, split in UN:
        at += 2 if split else 1
        done_of.append(at)
    FFN = ffn_order()
    UPP = len(FFN)
    ffn_index = {name: r for r, name in enumerate(FFN)}
    assert UPP % RAW == 0 and UPP % HIS == 0

    with ExitStack() as ctx:
        top = [(nc.sbuf_base + 63) // 64 * 64]

        def at_offset(name, shape, dt, offset):
            return nc.alloc_sbuf_tensor_at(name, shape, dt, offset=offset).ap()

        def size(shape, dt=F32):
            n = 2 if dt == BF16 else 4
            for s in shape[1:]:
                n *= s
            return (n + 31) // 32 * 32

        def sb(name, shape, dt=F32):
            t = at_offset(name, shape, dt, top[0])
            top[0] += size(shape, dt)
            return t

        raw_at = top[0]
        raw = sb("raw", [P, RAW, UNIT])
        w_lo = at_offset("w_lo", [P, RAW, UNIT], F32R, raw_at)
        w_hi = sb("w_hi", [P, HIS, UNIT], F32R)
        x = sb("x", [P, TILES, D])
        TH = sb("TH", [P, KC, SEQ], F32R)
        TL = sb("TL", [P, KC, SEQ], F32R)
        gate_a = sb("gate_a", [P, D])
        gate_f = sb("gate_f", [P, D])
        bias_at = top[0]
        bias = sb("bias", [P, DIFF_HEADS, 384])
        consts = sb("consts", [P, N_CONST])
        cols = sb("cols", [P, N_COLS])
        ones = sb("ones", [P, P])
        ada_p = sb("ada_p", [P, 2, NB])
        cond = sb("cond", [P, KC])
        cond_rep = sb("cond_rep", [P, KC, 32])
        mod = sb("mod", [P, DEPTH, 48])
        mod_a = sb("mod_a", [P, 2 * DEPTH, KC])
        h32_at = top[0]
        h32 = sb("h32", [P, 2, NB])
        tmp = at_offset("tmp", [P, 2, NB], F32, h32_at)
        rot = at_offset("rot", [P, 4, TILES * MLA_HEADS * HALF], F32, h32_at)
        ssq = sb("ssq", [P, 9, 8])
        ms = sb("ms", [P, 9, 8])
        rstd = sb("rstd", [P, 9, 8])
        neg_half = sb("neg_half", [P, 8])
        o_scale = sb("o_scale", [P, DEPTH, KC])
        lam_sum = sb("lam_sum", [P, 4])
        lam_exp = sb("lam_exp", [P, 4])
        neg_lam = sb("neg_lam", [P, DEPTH])
        pos_i = sb("pos_i", [P, 2], I32)
        posq = sb("posq", [P, 2])
        rb = sb("rb", [P, BUCKETS, DIFF_HEADS])
        rb_step = sb("rb_step", [P, BUCKETS - 1, DIFF_HEADS])
        ang = sb("ang", [P, TILES, HALF])
        turns = sb("turns", [P, TILES, HALF])
        ang_c = sb("ang_c", [P, TILES, HALF])
        cos = sb("cos", [P, TILES, HALF])
        sin = sb("sin", [P, TILES, HALF])
        neg_max = sb("neg_max", [P, 16, 2])
        psum_p = sb("psum_p", [P, 16, 2])
        rec = sb("rec", [P, 16, 2])
        rec_lam = sb("rec_lam", [P, 16, 2])
        region = top[0]

        top[0] = region
        mT_at = top[0]
        mT = sb("mT", [P, 2, 4, NB])
        xn = at_offset("xn", [P, TILES, D], F32, mT_at)
        dT = sb("dT", [P, 2, 2, NB])
        qk_at = top[0]
        qfull = sb("qfull", [P, TILES, MLA_HEADS * MD])
        kfull = sb("kfull", [P, TILES, MLA_HEADS, MD])
        o = at_offset("o", [P, TILES, D], F32, qk_at)
        posk_i = at_offset("posk_i", [P, SEQ], I32, top[0])
        vm = sb("vm", [P, TILES, NB])
        lam_rows = at_offset("lam_rows", [P, DEPTH, 4, QK], F32, top[0])
        dv = sb("dv", [P, TILES, NB])
        d_at = top[0]
        dq = sb("dq", [P, TILES, NB])
        dk = sb("dk", [P, TILES, NB])
        probs = at_offset("probs", [P, 3, 2, SEQ], F32, d_at)
        dist_all = at_offset("dist_all", [P, 384], F32, mT_at + 8192)
        posk = at_offset("posk", [P, SEQ], F32, d_at)
        dist = sb("dist", [P, 384], BF16)
        far = [at_offset("far0", [P, 2, 384], BF16, mT_at + 8192), at_offset("far1", [P, 2, 384], BF16, h32_at)]
        pT = [at_offset("pT0", [P, NB], F32, d_at + 6144), sb("pT1", [P, NB])]
        mq = at_offset("mq", [P, TILES, Q_RANK], F32, mT_at)
        mkv = at_offset("mkv", [P, TILES, MKV], F32, mT_at + size([P, TILES, Q_RANK]))
        end_attention = top[0]

        top[0] = region
        moe_out = sb("moe_out", [P, TILES, D])
        dense_aT = [at_offset(f"dense_aT{i}", [P, 2, 2 * SEQ], F32R, top[0] + i * 2 * 2 * SEQ * 4) for i in range(2)]
        xn_part = [sb(f"xn_part{i}", [P, TILES, D], BF16) for i in range(3)]
        xg32 = sb("xg32", [P, KC, SLOTS])
        logits = at_offset("logits", [P, SEQ], F32, top[0] - size([P, KC, SLOTS]))
        xn_rest = at_offset("xn_rest", [P, TILES, D], F32, top[0])
        xg_hi = sb("xg_hi", [P, KC, SLOTS], F32R)
        xg_lo = sb("xg_lo", [P, KC, SLOTS], F32R)
        y_hi = at_offset("y_hi", [P, D], F32R, bias_at)
        y_lo = sb("y_lo", [P, D], F32R)
        slot_of = sb("slot_of", [P, TILES, SLOTS], BF16)
        ident_b = sb("ident_b", [P, P], BF16)
        token_of = sb("token_of", [P, SEQ], F32R)
        silu = sb("silu", [P, 2, FB])
        act_f = sb("act_f", [P, 2, FB])
        expert_aT = [sb(f"expert_aT{i}", [P, 2, FB], F32R) for i in range(2)]
        aT = {1: expert_aT, 2: dense_aT}
        router_hi = sb("router_hi", [P, KC * EXPERTS], F32R)
        router_lo = sb("router_lo", [P, KC * EXPERTS], F32R)
        rl = sb("rl", [P, TILES, EXPERTS])
        top_v = sb("top_v", [P, TILES, 8])
        top_i = sb("top_i", [P, TILES, 8], U32)
        top_f = sb("top_f", [P, TILES, 8])
        top_w = sb("top_w", [P, TILES, 4])
        hot = sb("hot", [P, TILES, 2, EXPERTS])
        pos_t = sb("pos_t", [P, TILES, MAX_PASS + 1])
        sel_t = sb("sel_t", [P, TILES, MAX_PASS + 1])
        gate_t = sb("gate_t", [P, TILES, MAX_PASS + 2])
        count = sb("count", [P, EXPERTS])
        over = sb("over", [P, EXPERTS])
        rank = sb("rank", [P, EXPERTS + 1])
        over_hot = sb("over_hot", [P, MAX_OVER, EXPERTS])
        picked = sb("picked", [P, MAX_OVER, 1 + 3 * TILES, EXPERTS])
        pass_f = sb("pass_f", [P, MAX_PASS + 2])
        pass_i = sb("pass_i", [P, MAX_PASS + 2], I32)
        assert max(top[0], end_attention) <= nc.sbuf_usable_end, (top[0], end_attention, nc.sbuf_usable_end)

        bank = [ctx.enter_context(nc.psum_tensor(f"bank{i}", [P, NB], F32)) for i in range(8)]
        bank = [b[:] for b in bank]
        ADA = bank[7]

        def const(name):
            return consts[:, CONSTS[name][0]:CONSTS[name][1]]

        def col(name):
            return cols[:, COLS[name][0]:COLS[name][1]]

        ident, iota = const("ident"), const("iota")
        g_attn = col("g_attn").rearrange("p (l c) -> p l c", l=DEPTH)
        g_ffn = col("g_ffn").rearrange("p (l c) -> p l c", l=DEPTH)
        b_col = col("b_ada").rearrange("p (l c) -> p l c", l=DEPTH)
        q_gain = col("q_norm").rearrange("p (l c) -> p l c", l=DEPTH)
        kv_gain = col("kv_norm").rearrange("p (l c) -> p l c", l=DEPTH)

        def sem(name):
            return ctx.enter_context(nc.semaphore(name))

        raw_loaded = [sem(f"raw_loaded{i}") for i in range(RAW)]
        x_loaded, cols_loaded, small_loaded = sem("x_loaded"), sem("cols_loaded"), sem("small_loaded")
        gate_a_row, gate_f_row = sem("gate_a_row"), sem("gate_f_row")
        hi_ready, lo_ready, unit_done = sem("hi_ready"), sem("lo_ready"), sem("unit_done")
        silu_c, ones_ready, cond_ready = sem("silu_c"), sem("ones_ready"), sem("cond_ready")
        lam_summed, lam_exped, angles, trig = sem("lam_summed"), sem("lam_exped"), sem("angles"), sem("trig")
        ada_part, ada_comb, ada_used = sem("ada_part"), sem("ada_comb"), sem("ada_used")
        mod_ready = sem("mod_ready")
        ssq_ready, pool_step, rstd_ready, xn_ready = sem("ssq_ready"), sem("pool_step"), sem("rstd_ready"), sem("xn_ready")
        filled, evacuated, split_t = sem("filled"), sem("evacuated"), sem("split_t")
        kn_done, acc_act, x_added = sem("kn_done"), sem("acc_act"), sem("x_added")
        roped = sem("roped")
        scored, soft, exped, recip = sem("scored"), sem("soft"), sem("exped"), sem("recip")
        pT_filled, pT_ready, pv_done, o_ready = sem("pT_filled"), sem("pT_ready"), sem("pv_done"), sem("o_ready")
        silu_done, act_done = sem("silu_done"), sem("act_done")
        aT_filled, aT_hi_ready, aT_lo_ready = sem("aT_filled"), sem("aT_hi_ready"), sem("aT_lo_ready")
        dve_step = sem("dve_step")
        bias_started = sem("bias_started")
        router_split, xn_part_ready, routed, chosen, top_exp, placed_ps = (sem(n) for n in ("router_split", "xn_part_ready", "routed", "chosen", "top_exp", "placed_ps"))
        tables, slots_built, token_filled, token_ready = (sem(n) for n in ("tables", "slots_built", "token_filled", "token_ready"))
        gathered, xg_evac, xg_split = sem("gathered"), sem("xg_evac"), sem("xg_split")
        y_hi_ready, y_lo_ready, scattered, moe_added = (sem(n) for n in ("y_hi_ready", "y_lo_ready", "scattered", "moe_added"))
        silu_warm, logits_copied, moe_zero = sem("silu_warm"), sem("logits_copied"), sem("moe_zero")
        moe_in_x, final_ready, stored = sem("moe_in_x"), sem("final_ready"), sem("stored")

        acc_groups = []
        for l in range(DEPTH):
            acc_groups += [("in", l, gi) for gi in range(5)] + [("uq", l, 0), ("uq", l, 1), ("kn", l), ("v", l)]
            acc_groups += [("wo", l, 0), ("wo", l, 1)]
        acc_of = {g: q for q, g in enumerate(acc_groups)}
        WO_ADDED, FFN_ADDED = [(2, 4), (10, 12)], 8
        act_count, acc_free = 0, []
        for g in acc_groups:
            if g[0] == "wo":
                acc_free.append((x_added, WO_ADDED[g[1]][g[2]]))
            else:
                act_count += 1
                acc_free.append((acc_act, act_count))
        fills = []
        for l in range(DEPTH):
            fills += [("h", l, i) for i in range(4)] + [("mq", l, 0), ("mq", l, 1), ("ckv", l, 0)]
            fills += [("dT", l, qk, hp) for qk in range(2) for hp in range(2)]
            fills += [("mT", l, qk, hp) for qk in range(2) for hp in range(4)]
            fills += [("o", l, i) for i in range(4)] + [("f", l, i) for i in range(4)]
        fill_of = {f: i for i, f in enumerate(fills)}
        split_fills = [f for f in fills if f[0] in ("h", "mq", "ckv", "o", "f")]
        sfill_of = {f: i for i, f in enumerate(split_fills)}
        rms = {e: i for i, e in enumerate([("h", 0), ("lat", 0), ("sub", 0), ("f", 0), ("h", 1), ("lat", 1), ("sub", 1), ("f", 1), ("final", 1)])}
        ada_groups = [(0, g) for g in range(12)] + [(1, g) for g in range(12)]
        steps = []
        for kind, hp in (("diff", 0), ("mla", 0), ("mla", 1), ("mla", 2), ("diff", 1), ("mla", 3)):
            steps += [(kind, hp, t, m) for t in range(TILES) for m in range(2 if kind == "diff" else 1)]
        DIFF_STEPS = 1 + max(s for s, step in enumerate(steps) if step[0] == "diff")
        NS = len(steps)

        def n_keys(s):
            return P * (steps[s][2] + 1)

        def wait(eng, s, value):
            if not isinstance(value, int) or value > 0:
                eng.wait_ge(s, value)

        class Unit:

            def __init__(self, name, p=None):
                if p is None:
                    self.n = unit_of[name]
                    self.slot, self.cols = self.n % RAW, UN[self.n][1]
                    self.loaded = 16 * (self.n // RAW + 1)
                    self.done = done_of[self.n]
                    if UN[self.n][2]:
                        h = split_of[name]
                        self.hi_slot = h % HIS
                        self.part_done = (self.done - 1, self.done)
                        self.ready = (2 * h + 1, 2 * h + 2)
                        before = done_of[split_units[h - HIS]] if h >= HIS else 0
                        self.hi_free = (before - 1, before)
                else:
                    r = name
                    n = N_STATIC + r
                    self.slot, self.cols = n % RAW, UNIT
                    self.loaded = p * (16 * UPP // RAW) + 16 * (n // RAW + 1)
                    self.done = p * (2 * UPP) + (done_of[-1] + 2 * (r + 1))
                    self.part_done = (self.done - 1, self.done)
                    h = N_SPLIT + r
                    self.hi_slot = h % HIS
                    self.ready = (p * (2 * UPP) + (2 * h + 1), p * (2 * UPP) + (2 * h + 2))
                    self.hi_free = (self.done - 2 * HIS - 1, self.done - 2 * HIS)
                cut = 2 * self.cols // 3 if p is None and name[0] == "uq" else self.cols // 2
                self.cut = cut
                self.parts = [(slice(a, b), slice(part * UNIT // 2, part * UNIT // 2 + b - a))
                              for part, (a, b) in enumerate(((0, cut), (cut, self.cols)))]

            def hi_cols(self, cs):
                shift = UNIT // 2 - self.cut if cs.start >= self.cut else 0
                return slice(cs.start + shift, cs.stop + shift)

        def act_hi(eng, u):
            eng.wait_ge(raw_loaded[u.slot], u.loaded)
            for part, (cs, hs) in enumerate(u.parts):
                wait(eng, unit_done, u.hi_free[part])
                nc.scalar.activation(w_hi[:, u.hi_slot, hs], raw[:, u.slot, cs], ACT.Copy).then_inc(hi_ready, 1)

        def dve_lo(eng, u):
            for part, (cs, hs) in enumerate(u.parts):
                eng.wait_ge(hi_ready, u.ready[part])
                nc.vector.tensor_tensor(w_lo[:, u.slot, cs], raw[:, u.slot, cs],
                                        w_hi[:, u.hi_slot, hs].bitcast(F32), ALU.subtract).then_inc(lo_ready, 1)

        def split_unit(h):
            return Unit(UN[split_units[h]][0])

        def acc_last(group):
            kind, l, *n = group
            return Unit({"in": ("in", l, *n, 1), "uq": ("uq", l, *n), "v": ("ukv", l), "wo": ("wo", l, *n, 1)}[kind])

        WO_STEPS = (11, 12, 13)
        H_WO = [split_of[("wo", l, 0, 0)] for l in range(DEPTH)]

        block = ctx.enter_context(nc.Block())

        @block.sync
        def _(sp):
            sp.dma_start(cols[:], cols_in).then_inc(cols_loaded, 16)
            sp.dma_start(consts[:], consts_in).then_inc(small_loaded, 16)
            sp.dma_start(pos_i[:], pos_cols).then_inc(small_loaded, 16)
            sp.dma_start(posk_i[:], pos_in.broadcast_to([P, SEQ])).then_inc(small_loaded, 16)
            sp.dma_start(rb[:].rearrange("p b h -> p (b h)"),
                         rel_bias.rearrange("(o b) h -> o (b h)", o=1).broadcast_to([P, BUCKETS * DIFF_HEADS])).then_inc(small_loaded, 16)
            sp.dma_start(lam_rows[:].rearrange("p l a d -> p (l a d)"),
                         diff_lambda.rearrange("(o l) a d -> o (l a d)", o=1).broadcast_to([P, DEPTH * 4 * QK])).then_inc(small_loaded, 16)
            sp.dma_start(x[:], x_in.rearrange("o (t p) n -> p (o t) n", p=P)).then_inc(x_loaded, 16)
            for n, (name, c, _) in enumerate(UN):
                if name == ("A", 3):
                    sp.wait_ge(x_added, WO_ADDED[0][1])
                    sp.dma_start(gate_a[:], b_ada[1:2, 2 * D:3 * D].broadcast_to([P, D])).then_inc(gate_a_row, 16)
                if name == ("wo", 1, 0, 0):
                    sp.wait_ge(x_added, FFN_ADDED)
                    sp.dma_start(gate_f[:], b_ada[1:2, 5 * D:6 * D].broadcast_to([P, D])).then_inc(gate_f_row, 16)
                if n >= RAW:
                    sp.wait_ge(unit_done, done_of[n - RAW])
                sp.dma_start(raw[:, n % RAW, 0:c],
                             w_static[offset[n]:offset[n] + P * c].rearrange("(p c) -> p c", p=P)).then_inc(raw_loaded[n % RAW], 16)

            def expert_units(p, expert):
                for r in range(UPP):
                    n = N_STATIC + r
                    if r >= RAW:
                        sp.wait_ge(unit_done, Unit(r - RAW, p).done)
                    elif isinstance(p, int):
                        sp.wait_ge(unit_done, done_of[n - RAW])
                    else:
                        sp.wait_ge(unit_done, p * (2 * UPP) + (done_of[-1] + 2 * (r + 1 - RAW)))
                    sp.dma_start(raw[:, n % RAW, :], w_moe[bass.ds(expert, 1), r].rearrange("e p c -> p (e c)"))\
                        .then_inc(raw_loaded[n % RAW], 16)

            expert_units(0, 0)
            sp.wait_ge(tables, 1)
            n_pass = sp.value_load(pass_i[0:1, MAX_PASS + 1:MAX_PASS + 2], min_val=EXPERTS, max_val=MAX_PASS)
            with sp.Fori(1, n_pass) as p:
                expert = sp.value_load(pass_i[0:1, bass.ds(p, 1)], min_val=0, max_val=EXPERTS - 1)
                expert_units(p, expert)
            for r in range(2):
                n = N_STATIC + r
                sp.wait_ge(unit_done, n_pass * (2 * UPP) + (done_of[-1] + 2 * (r + 1 - RAW)))
                sp.dma_start(raw[:, n % RAW, :], w_moe[0, r]).then_inc(raw_loaded[n % RAW], 16)
            sp.wait_ge(x_added, WO_ADDED[1][1])
            sp.dma_start(gate_a[:], g_final.unsqueeze(0).broadcast_to([P, D])).then_inc(gate_a_row, 16)
            for t in range(TILES):
                sp.wait_ge(final_ready, t + 1)
                sp.dma_start(out[0, t * P:(t + 1) * P, :], xn[:, t, :]).then_inc(stored, 16)
            sp.wait_ge(stored, 16 * TILES)

        @block.gpsimd
        def _(pool):
            nc.gpsimd.memset(neg_half[:], -0.5).then_inc(pool_step, 1)
            pool.wait_ge(pool_step, 1)
            done = 1
            for (kind, l), r in rms.items():
                if kind == "final":
                    pool.wait_ge(xn_part_ready, 2)
                    nc.gpsimd.memset(moe_out[:], 0.0).then_inc(moe_zero, 1)
                parts = {"lat": [(0, 2, Q_RANK), (2, 4, KV_RANK)], "sub": [(0, 8, 2 * QK)]}.get(kind, [(0, 2, D)])
                pool.wait_ge(ssq_ready, r + 1)
                if (kind, l) == ("h", 1) or kind == "f":
                    nc.gpsimd.tensor_tensor(ssq[:, r, 0:2], ssq[:, r, 0:2], ssq[:, r, 2:4], ALU.add).then_inc(pool_step, 1)
                    done += 1
                    pool.wait_ge(pool_step, done)
                for a, b, width in parts:
                    nc.gpsimd.tensor_scalar(ms[:, r, a:b], ssq[:, r, a:b], 1.0 / width, EPS, ALU.mult, ALU.add).then_inc(pool_step, 1)
                    done += 1
                pool.wait_ge(pool_step, done)
                b = parts[-1][1]
                nc.gpsimd.tensor_tensor(rstd[:, r, 0:b], ms[:, r, 0:b], neg_half[:, 0:b], ALU.pow).then_inc(rstd_ready, 1)

        @block.scalar
        def _(act):
            act.wait_ge(cols_loaded, 16)
            nc.scalar.activation(cond[:], col("c"), ACT.Silu).then_inc(silu_c, 1)
            act.wait_ge(small_loaded, 80)
            act.dma_start(gate_a[:], b_ada[0:1, 2 * D:3 * D].broadcast_to([P, D])).then_inc(gate_a_row, 16)
            act.dma_start(gate_f[:], b_ada[0:1, 5 * D:6 * D].broadcast_to([P, D])).then_inc(gate_f_row, 16)
            act.wait_ge(lam_summed, 4)
            nc.scalar.activation(lam_exp[:], lam_sum[:], ACT.Exp).then_inc(lam_exped, 1)
            act.wait_ge(angles, 1)
            nc.scalar.activation(sin[:], ang[:], ACT.Sin).then_inc(trig, 1)
            nc.scalar.activation(cos[:], ang_c[:], ACT.Sin).then_inc(trig, 1)

            def squares(event, parts, last=True):
                for i, (src, dst, c) in enumerate(parts):
                    ins = nc.scalar.activation(dst, src, ACT.Square, accum_out=ssq[:, rms[event], c:c + 1])
                if last:
                    ins.then_inc(ssq_ready, 1)

            def x_squares(event):
                squares(event, [(x[:, t, :], xn[:, t, :], t) for t in range(TILES)])

            def quarter_squares(event, quarters):
                for added, t, half in quarters:
                    act.wait_ge(x_added, added)
                    cs = slice(half * NB, (half + 1) * NB)
                    ins = nc.scalar.activation(xn[:, t, cs], x[:, t, cs], ACT.Square, accum_out=ssq[:, rms[event], 2 * half + t:2 * half + t + 1])
                ins.then_inc(ssq_ready, 1)

            def ada_partials(G):
                act.wait_ge(unit_done, Unit(("ada", *ada_groups[G], 1)).done)
                wait(act, ada_comb, G - 1)
                nc.scalar.activation(ada_p[:, G % 2, :], ADA, ACT.Copy).then_inc(ada_part, 1)

            def evac_split(fill, scale, shift):
                f, s = fill_of[fill], sfill_of[fill]
                act.wait_ge(filled, f + 1)
                wait(act, split_t, 2 * (s - 1))
                for i in range(len(scale)):
                    ins = nc.scalar.activation(h32[:, s % 2, i * SEQ:(i + 1) * SEQ], bank[4 + f % 3][:, i * SEQ:(i + 1) * SEQ],
                                               ACT.Identity, bias=shift[i] if shift else 0.0, scale=scale[i])
                ins.then_inc(evacuated, 1)

            def evac_copy(fill, dst, rows=P):
                f = fill_of[fill]
                act.wait_ge(filled, f + 1)
                nc.scalar.activation(dst, bank[4 + f % 3][0:rows, :], ACT.Copy).then_inc(evacuated, 1)

            def evac_h(kind, l):
                k = 2 * l + (kind == "f")
                base = 24 if kind == "f" else 0
                act.wait_ge(mod_ready, k + 1)
                for i in range(4):
                    c = [2 * i, 2 * i + 1]
                    evac_split((kind, l, i), [mod_a[:, k, j:j + 1] for j in c], [mod[:, l, base + j:base + j + 1] for j in c])

            def evac_acc(group, dst0, dst1, width, view=None):
                q = acc_of[group]
                if group[0] == "kn":
                    act.wait_ge(kn_done, group[1] + 1)
                else:
                    act.wait_ge(unit_done, acc_last(group).done)
                for t, dst in ((0, dst0), (1, dst1)):
                    src = bank[2 * (q % 2) + t][:, 0:width]
                    ins = nc.scalar.activation(dst, view(src) if view else src, ACT.Copy)
                ins.then_inc(acc_act, 1)

            def head_squares(hp):
                return [(o[:, t, h * P:(h + 1) * P], h32[:, 1 - hp, (2 * t + h % 2) * P:(2 * t + h % 2 + 1) * P], 4 * t + h)
                        for t in range(TILES) for h in (2 * hp, 2 * hp + 1)]

            def attention(l):
                def copy_pT(s):
                    S = NS * l + s
                    act.wait_ge(pT_filled, S + 1)
                    wait(act, pv_done, S - 1)
                    w = 2 * n_keys(s)
                    nc.scalar.activation(pT[s % 2][:, 0:w], bank[3 + s % 2][:, 0:w], ACT.Copy).then_inc(pT_ready, 1)

                first = 4 if l == 0 else 22
                n_ada = 8 if l == 0 else 2
                for s in range(NS + 2):
                    S = NS * l + s
                    if s >= 2 and s % 2 == 0 and s // 2 <= n_ada:
                        ada_partials(first + s // 2 - 1)
                    if s >= 2:
                        copy_pT(s - 2)
                    if s < NS:
                        act.wait_ge(soft, 2 * (S + 1))
                        n = n_keys(s)
                        for hh in range(2):
                            nc.scalar.activation(probs[:, s % 3, hh, 0:n], probs[:, s % 3, hh, 0:n], ACT.Exp,
                                                 bias=neg_max[:, s, hh:hh + 1], accum_out=psum_p[:, s, hh:hh + 1]).then_inc(exped, 1)
                    if s == 9:
                        act.wait_ge(o_ready, NS * l + 4)
                        squares(("sub", l), head_squares(0), last=False)
                    if s in WO_STEPS:
                        act_hi(act, split_unit(H_WO[l] + WO_STEPS.index(s)))

            def layer_attention(l):
                h0 = split_of[("in", l, 0, 0)]
                if l == 0:
                    act.wait_ge(x_loaded, 16)
                    x_squares(("h", 0))
                    for G in range(4):
                        ada_partials(G)
                else:
                    act_hi(act, split_unit(h0 + 2))
                    quarter_squares(("h", 1), [(FFN_ADDED - 3 + 2 * t + half, t, half) for t in range(TILES) for half in range(2)])
                evac_h("h", l)
                if l == 0:
                    for h in range(3):
                        act_hi(act, split_unit(h))
                for gi, (name, _, w) in enumerate(IN_GROUPS):
                    act_hi(act, split_unit(h0 + 2 * gi + 3))
                    dst = {"mq": mq, "mkv": mkv, "dq": dq, "dk": dk, "dv": dv}[name]
                    evac_acc(("in", l, gi), dst[:, 0, :], dst[:, 1, :], w)
                    act_hi(act, split_unit(h0 + 2 * gi + 4))
                    if name == "mkv":
                        act.wait_ge(acc_act, acc_free[acc_of[("in", l, 1)]][1])
                        squares(("lat", l), [(mq[:, t, :], h32[:, t, 0:Q_RANK], t) for t in range(TILES)] +
                                [(mkv[:, t, 0:KV_RANK], ada_p[:, t, 0:KV_RANK], 2 + t) for t in range(TILES)])
                evac_split(("mq", l, 0), [q_gain[:, l, i:i + 1] for i in (0, 1)], None)
                evac_split(("mq", l, 1), [q_gain[:, l, 2:3]], None)
                evac_split(("ckv", l, 0), [kv_gain[:, l, i:i + 1] for i in (0, 1)], None)
                for qk in range(2):
                    for hp in range(2):
                        evac_copy(("dT", l, qk, hp), dT[:, qk, hp, :])
                for u in range(2):
                    evac_acc(("uq", l, u), qfull[:, 0, u * 384:(u + 1) * 384], qfull[:, 1, u * 384:(u + 1) * 384], 384)
                evac_acc(("kn", l), kfull[:, 0, :, 0:QK], kfull[:, 1, :, 0:QK], NB,
                         lambda s: s.rearrange("p (h d) -> p h d", d=QK))
                evac_acc(("v", l), vm[:, 0, :], vm[:, 1, :], NB)
                for qk in range(2):
                    for hp in range(4):
                        evac_copy(("mT", l, qk, hp), mT[0:MD, qk, hp, :], MD)
                attention(l)
                act.wait_ge(o_ready, NS * l + DIFF_STEPS)
                squares(("sub", l), head_squares(1))
                for i in range(4):
                    evac_split(("o", l, i), [o_scale[:, l, j:j + 1] for j in (2 * i, 2 * i + 1)], None)
                act_hi(act, split_unit(H_WO[l] + 3))
                for i in range(3 if l == 0 else 0):
                    act_hi(act, split_unit(H_WO[l] + 4 + i))
                if l == 1:
                    for i in range(2):
                        act_hi(act, Unit(i, 0))
                quarter_squares(("f", l), [(WO_ADDED[l][half] - 1 + t, t, half) for half in range(2) for t in range(TILES)])
                if l == 1:
                    act.wait_ge(xn_ready, 8)
                    nc.scalar.activation(xn_part[0][:], xn[:], ACT.Copy).then_inc(xn_part_ready, 1)
                evac_h("f", l)

            def silu_part(j, tiles, up, base_s):
                act.wait_ge(unit_done, up.done)
                wait(act, act_done, base_s + tiles * j)
                for t in range(tiles):
                    b = bank[4 + t] if tiles == 2 else bank[2 + j % 2]
                    nc.scalar.activation(silu[:, t, :], b[:, 0:FB], ACT.Silu).then_inc(silu_done, 1)

            def aT_hi_part(j, tiles, base_h):
                act.wait_ge(aT_filled, base_h + (j + 1))
                b = bank[6 if tiles == 2 else 4]
                w = 2 * P * tiles
                nc.scalar.activation(aT[tiles][0][:, j % 2, 0:w], b[:, 0:w], ACT.Copy).then_inc(aT_hi_ready, 1)

            layer_attention(0)
            h0 = split_of[("A", 0)]
            for j in range(BLOCKS):
                if j:
                    aT_hi_part(j - 1, 2, 0)
                act_hi(act, split_unit(h0 + ffn_index[("A", j)] + 3))
                silu_part(j, 2, Unit(("B", j)), 0)
                act_hi(act, split_unit(h0 + ffn_index[("B", j)] + 3))
                if j:
                    act_hi(act, split_unit(h0 + ffn_index[("C", j - 1)] + 3))
                if j < 10:
                    ada_partials(12 + j)
            aT_hi_part(BLOCKS - 1, 2, 0)
            layer_attention(1)

            act.wait_ge(routed, 1)
            nc.scalar.activation(logits[0:EXPERTS, :], bank[7][0:EXPERTS, 0:SEQ], ACT.Copy).then_inc(logits_copied, 1)
            act.wait_ge(xn_part_ready, 2)
            nc.scalar.activation(xn_part[1][:], xn_rest[:], ACT.Copy).then_inc(xn_part_ready, 1)
            act.wait_ge(chosen, 1)
            for t in range(TILES):
                nc.scalar.activation(top_w[:, t, 1:2], top_v[:, t, 1:2], ACT.Exp, bias=top_w[:, t, 0:1]).then_inc(top_exp, 1)

            def evac_gathered(base):
                for b in range(2):
                    act.wait_ge(gathered, base * 2 + (b + 1))
                    if b == 0:
                        wait(act, xg_split, base * 2)
                    for c in range(4 * b, 4 * b + 4):
                        ins = nc.scalar.activation(xg32[:, c, :], bank[5 + b][:, (c % 4) * P:(c % 4 + 1) * P], ACT.Identity,
                                                   bias=mod[:, 1, 24 + c:25 + c], scale=mod_a[:, 3, c:c + 1])
                    ins.then_inc(xg_evac, 1)

            act.wait_ge(moe_zero, 1)
            nc.scalar.activation(token_of[:], moe_out[:, 0, 0:SEQ], ACT.Copy).then_inc(token_ready, 1)
            nc.scalar.activation(y_hi[:], moe_out[:, 0, :], ACT.Copy).then_inc(y_hi_ready, 2)
            nc.scalar.activation(y_lo[:], moe_out[:, 0, :], ACT.Copy).then_inc(y_lo_ready, 2)
            nc.scalar.activation(act_f[:, 1, 0:1], cond[:, 0:1], ACT.Silu).then_inc(silu_warm, 1)
            evac_gathered(0)
            act.wait_ge(tables, 1)
            n_pass = act.value_load(pass_i[0:1, MAX_PASS + 1:MAX_PASS + 2], min_val=EXPERTS, max_val=MAX_PASS)
            with act.Fori(0, n_pass) as p:
                base_h = p * BLOCKS + BLOCKS
                base_s = p * BLOCKS + 2 * BLOCKS
                act_hi(act, Unit(2, p))
                for j in range(BLOCKS):
                    if j:
                        aT_hi_part(j - 1, 1, base_h)
                    if ffn_index[("A", j)] + 3 < UPP:
                        act_hi(act, Unit(ffn_index[("A", j)] + 3, p))
                    silu_part(j, 1, Unit(ffn_index[("B", j)], p), base_s)
                    if ffn_index[("B", j)] + 3 < UPP:
                        act_hi(act, Unit(ffn_index[("B", j)] + 3, p))
                    if j and ffn_index[("C", j - 1)] + 3 < UPP:
                        act_hi(act, Unit(ffn_index[("C", j - 1)] + 3, p))
                    if j == 4:
                        act.wait_ge(token_filled, p + 1)
                        nc.scalar.activation(token_of[:], bank[7][:, 0:SEQ], ACT.Copy).then_inc(token_ready, 1)
                    if j == 7:
                        evac_gathered(p + 1)
                act_hi(act, Unit(UPP, p))
                aT_hi_part(BLOCKS - 1, 1, base_h)
                act_hi(act, Unit(UPP + 1, p))
                act.wait_ge(unit_done, Unit(ffn_index[("C", BLOCKS - 1)], p).done)
                for b in range(2):
                    nc.scalar.activation(y_hi[:, b * NB:(b + 1) * NB], bank[b], ACT.Copy).then_inc(y_hi_ready, 1)
            for t in range(TILES):
                act.wait_ge(moe_in_x, t + 1)
                ins = nc.scalar.activation(xn[:, t, :], x[:, t, :], ACT.Square, accum_out=ssq[:, rms[("final", 1)], t:t + 1])
            ins.then_inc(ssq_ready, 1)

        @block.vector
        def _(dve):
            steps_done = [0]

            def link(ins):
                steps_done[0] += 1
                ins.then_inc(dve_step, 1)
                dve.wait_ge(dve_step, steps_done[0])

            def mark(ins):
                steps_done[0] += 1
                ins.then_inc(dve_step, 1)
                return steps_done[0]

            mark(nc.vector.memset(ones[:], 1.0))
            dve.wait_ge(silu_c, 1)
            nc.vector.tensor_copy(cond_rep[:], cond[:].unsqueeze(2).to_broadcast([P, KC, 32])).then_inc(cond_ready, 1)
            dve.wait_ge(small_loaded, 80)
            mark(nc.vector.tensor_copy(posq[:], pos_i[:]))
            link(nc.vector.tensor_copy(posk[:], posk_i[:]))
            for t, (a, b) in enumerate(((0, P), (P, 384))):
                link(nc.vector.tensor_scalar(dist_all[:, a:b], posk[:, 0:b - a], posq[:, t:t + 1], -1.0, ALU.subtract, ALU.mult))
                link(nc.vector.tensor_scalar(dist[:, a:b], dist_all[:, a:b], 256.0, 0.0, ALU.min, ALU.max))
            link(nc.vector.tensor_tensor(rb_step[:], rb[:, 1:BUCKETS, :], rb[:, 0:BUCKETS - 1, :], ALU.subtract))
            for h in range(DIFF_HEADS):
                ins = nc.vector.tensor_scalar(bias[:, h, :], const("mask"), rb[:, 0, h:h + 1], None, ALU.add)
            ins.then_inc(bias_started, 1)
            for l in range(DEPTH):
                for i in range(2):
                    nc.vector.tensor_tensor_reduce(out=rot[:, 2 * l + i, 0:QK], in0=lam_rows[:, l, 2 * i, :], in1=lam_rows[:, l, 2 * i + 1, :],
                                                   scale=1.0, scalar=0.0, op0=ALU.mult, op1=ALU.add,
                                                   accum_out=lam_sum[:, 2 * l + i:2 * l + i + 1]).then_inc(lam_summed, 1)
            for t in range(TILES):
                link(nc.vector.tensor_scalar(ang[:, t, :], const("freq"), posq[:, t:t + 1], None, ALU.mult))
            magic = 1.5 * 2.0 ** 23
            link(nc.vector.tensor_scalar(turns[:], ang[:], 1.0 / (2 * math.pi), magic, ALU.mult, ALU.add))
            link(nc.vector.tensor_scalar(turns[:], turns[:], magic, None, ALU.subtract))
            c1 = 6.28125
            c2 = 0.0019340515136718750
            c3 = 2 * math.pi - c1 - c2
            for c in (c1, c2, c3):
                link(nc.vector.scalar_tensor_tensor(ang[:], turns[:], -c, ang[:], ALU.mult, ALU.add))
            link(nc.vector.tensor_scalar(ang_c[:], ang[:], math.pi / 2, None, ALU.add))
            link(nc.vector.tensor_scalar(turns[:], ang_c[:], math.pi, -2 * math.pi, ALU.is_gt, ALU.mult))
            link(nc.vector.tensor_tensor(ang_c[:], ang_c[:], turns[:], ALU.add))
            lim = 3.1415925
            link(nc.vector.tensor_scalar(ang_c[:], ang_c[:], lim, -lim, ALU.min, ALU.max))
            nc.vector.tensor_scalar(ang[:], ang[:], lim, -lim, ALU.min, ALU.max).then_inc(angles, 1)
            dve.wait_ge(lam_exped, 1)
            for l in range(DEPTH):
                link(nc.vector.tensor_tensor(neg_lam[:, l:l + 1], lam_exp[:, 2 * l + 1:2 * l + 2], lam_exp[:, 2 * l:2 * l + 1], ALU.subtract))
                link(nc.vector.tensor_scalar(neg_lam[:, l:l + 1], neg_lam[:, l:l + 1], LAM_INIT[l], None, ALU.subtract))
                mark(nc.vector.memset(o_scale[:, l, 4:8], 1.0))
                mark(nc.vector.tensor_scalar(o_scale[:, l, 0:4], ones[:, 0:4], col("subln")[:, l:l + 1], 1.0 - LAM_INIT[l], ALU.mult, ALU.mult))

            last_far = [0, 0]
            last_bias = [0] * DIFF_HEADS

            def bias_steps():
                dve.wait_ge(bias_started, 1)
                for heads, buckets in ((range(4), range(BIAS_SPLIT)), (range(2), range(BIAS_SPLIT, BUCKETS - 1)),
                                       (range(2, 4), range(BIAS_SPLIT, BUCKETS - 1))):
                    for b in buckets:
                        reached = far[in_attention[0]][:, b % 2, :]
                        wait(dve, dve_step, last_far[b % 2])
                        link(nc.vector.tensor_scalar(reached, dist[:], float(THRESHOLDS[b]), None, ALU.is_ge))
                        for h in heads:
                            wait(dve, dve_step, last_bias[h])
                            last_bias[h] = mark(nc.vector.scalar_tensor_tensor(
                                bias[:, h, :], reached, rb_step[:, b, h:h + 1], bias[:, h, :], ALU.mult, ALU.add))
                        last_far[b % 2] = last_bias[heads[-1]]
                        bias_count[0] += 1
                        yield

            bias_work = bias_steps()
            bias_count, in_attention = [0], [0]

            def bias_more(n, until=2 * (BUCKETS - 1) - BIAS_SPLIT):
                for _ in range(min(n, until - bias_count[0])):
                    next(bias_work)

            def ada_take(G):
                l, g = ada_groups[G]
                dve.wait_ge(ada_comb, G + 1)
                if g in (4, 5, 10, 11):
                    gate, row = (gate_a, gate_a_row) if g < 6 else (gate_f, gate_f_row)
                    dve.wait_ge(row, 16 * (l + 1))
                    half = gate[:, (g % 2) * NB:(g % 2 + 1) * NB]
                    nc.vector.scalar_tensor_tensor(half, ADA, 1.0, half, ALU.add, ALU.add).then_inc(ada_used, 1)
                else:
                    nc.vector.tensor_tensor(mod[:, l, 4 * g:4 * g + 4], ADA[:, 0:4], b_col[:, l, 4 * g:4 * g + 4], ALU.add).then_inc(ada_used, 1)
                if g in (3, 9):
                    k = 2 * l + (g == 9)
                    dve.wait_ge(ada_used, G + 1)
                    base, gain = (8, g_attn) if g == 3 else (32, g_ffn)
                    nc.vector.scalar_tensor_tensor(mod_a[:, k, :], mod[:, l, base:base + 8], 1.0, gain[:, l, :], ALU.add, ALU.mult).then_inc(mod_ready, 1)

            def normalise_x(event):
                r = rms[event]
                dve.wait_ge(rstd_ready, r + 1)
                for t in range(TILES):
                    ins = nc.vector.tensor_scalar(xn[:, t, :], x[:, t, :], rstd[:, r, t:t + 1], None, ALU.mult)
                ins.then_inc(xn_ready, 1)

            def split_fill(fill, chunk, n):
                f, s = fill_of[fill], sfill_of[fill]
                dve.wait_ge(evacuated, f + 1)
                src = h32[:, s % 2, 0:n * SEQ]
                hi = TH[:, chunk:chunk + n, :].rearrange("p c t -> p (c t)")
                lo = TL[:, chunk:chunk + n, :].rearrange("p c t -> p (c t)")
                nc.vector.tensor_copy(hi, src).then_inc(split_t, 1)
                dve.wait_ge(split_t, 2 * s + 1)
                nc.vector.tensor_tensor(lo, src, hi.bitcast(F32), ALU.subtract).then_inc(split_t, 1)

            def rope(src1, src2, dst1, dst2, shape):
                c, s = cos[:], sin[:]
                if len(shape) == 4:
                    c, s = (a.unsqueeze(2).to_broadcast(shape) for a in (c, s))
                n = shape[1] * shape[-1] * (shape[2] if len(shape) == 4 else 1)

                def part(i):
                    v = rot[:, i, 0:n]
                    if len(shape) == 4:
                        return v.rearrange("p (t h i) -> p t h i", t=shape[1], h=shape[2])
                    return v.rearrange("p (t i) -> p t i", t=shape[1])

                for i, (a, b) in enumerate(((src1, c), (src2, s), (src2, c), (src1, s))):
                    last = mark(nc.vector.tensor_tensor(part(i), a, b, ALU.mult))
                dve.wait_ge(dve_step, last)
                mark(nc.vector.tensor_tensor(dst1, part(0), part(1), ALU.subtract))
                return nc.vector.tensor_tensor(dst2, part(2), part(3), ALU.add)

            def attention(l):
                def take_o(s):
                    S = NS * l + s
                    kind, hp, t, m = steps[s]
                    b = bank[5 + s % 2]
                    dve.wait_ge(recip, S + 1)
                    if kind == "diff" and m == 1:
                        link(nc.vector.tensor_scalar(rec_lam[:, s, :], rec[:, s, :], neg_lam[:, l:l + 1], None, ALU.mult))
                    dve.wait_ge(pv_done, S + 1)
                    if kind == "mla":
                        dst = o[:, t, NB + hp * P:NB + (hp + 1) * P].rearrange("p (a d) -> p a d", a=2)
                        nc.vector.tensor_tensor(dst, b[:, 0:P].rearrange("p (a d) -> p a d", a=2),
                                                rec[:, s, :].unsqueeze(2).to_broadcast([P, 2, QK]), ALU.mult).then_inc(o_ready, 1)
                    elif m == 0:
                        dst = o[:, t, hp * 2 * P:(hp + 1) * 2 * P].rearrange("p (a d) -> p a d", a=2)
                        nc.vector.tensor_tensor(dst, b[:, 0:2 * P].rearrange("p (a d) -> p a d", a=2),
                                                rec[:, s, :].unsqueeze(2).to_broadcast([P, 2, P]), ALU.mult).then_inc(o_ready, 1)
                    else:
                        dve.wait_ge(o_ready, S)
                        for hh in range(2):
                            dst = o[:, t, (2 * hp + hh) * P:(2 * hp + hh + 1) * P]
                            ins = nc.vector.scalar_tensor_tensor(dst, b[:, hh * P:(hh + 1) * P], rec_lam[:, s, hh:hh + 1], dst, ALU.mult, ALU.add)
                        ins.then_inc(o_ready, 1)

                first = 4 if l == 0 else 22
                n_ada = 8 if l == 0 else 2
                for s in range(NS + 3):
                    S = NS * l + s
                    if s < NS:
                        kind, hp, t, m = steps[s]
                        n = n_keys(s)
                        b = bank[s % 3].rearrange("p (a k) -> p a k", a=2)[:, :, 0:n]
                        at = 0 if t == 0 else P
                        if (l, kind, hp, t, m) == (0, "diff", 1, 0, 0):
                            bias_more(BUCKETS)
                            dve.wait_ge(dve_step, max(last_bias))
                        if kind == "diff":
                            add, scale = bias[:, 2 * hp:2 * hp + 2, at:at + n], QK ** -0.5
                        else:
                            add, scale = const("mask")[:, at:at + n].unsqueeze(1).to_broadcast([P, 2, n]), MD ** -0.5
                        dve.wait_ge(scored, S + 1)
                        if s >= 3:
                            dve.wait_ge(pT_filled, S - 2)
                        w = probs[:, s % 3, :, 0:n]
                        nc.vector.scalar_tensor_tensor(w, b, scale, add, ALU.mult, ALU.add).then_inc(soft, 1)
                        dve.wait_ge(soft, 2 * S + 1)
                        nc.vector.tensor_reduce(neg_max[:, s, :], w, AX.X, ALU.max, negate=True).then_inc(soft, 1)
                    if l == 0:
                        in_attention[0] = 1
                        if s == 0:
                            dve.wait_ge(roped, 1)
                        bias_more(BIAS_IN_STEP)
                    if 1 <= s <= NS:
                        dve.wait_ge(exped, 2 * S)
                        nc.vector.reciprocal(rec[:, s - 1, :], psum_p[:, s - 1, :]).then_inc(recip, 1)
                    if s >= 2 and s % 2 == 0 and s // 2 <= n_ada:
                        ada_take(first + s // 2 - 1)
                    if s >= 3:
                        take_o(s - 3)
                    if s - 1 in WO_STEPS:
                        dve_lo(dve, split_unit(H_WO[l] + WO_STEPS.index(s - 1)))

            def layer_attention(l):
                h0 = split_of[("in", l, 0, 0)]
                if l == 1:
                    dve_lo(dve, split_unit(h0 + 2))
                normalise_x(("h", l))
                if l == 0:
                    bias_more(BIAS_AT[0])
                    for G in range(4):
                        ada_take(G)
                        bias_more(BIAS_AT[1 + G])
                for i in range(4):
                    split_fill(("h", l, i), 2 * i, 2)
                if l == 0:
                    for h in range(3):
                        dve_lo(dve, split_unit(h))
                for gi in range(5):
                    for i in (3, 4):
                        dve_lo(dve, split_unit(h0 + 2 * gi + i))
                        bias_more(BIAS_AT_UNIT)
                    if gi == 2:
                        r = rms[("lat", l)]
                        dve.wait_ge(rstd_ready, r + 1)
                        for t in range(TILES):
                            nc.vector.tensor_scalar(mq[:, t, :], mq[:, t, :], rstd[:, r, t:t + 1], None, ALU.mult)
                            ins = nc.vector.tensor_scalar(mkv[:, t, 0:KV_RANK], mkv[:, t, 0:KV_RANK], rstd[:, r, 2 + t:3 + t], None, ALU.mult)
                        ins.then_inc(xn_ready, 1)
                split_fill(("mq", l, 0), 0, 2)
                split_fill(("mq", l, 1), 2, 1)
                split_fill(("ckv", l, 0), 4, 2)
                bias_more(BUCKETS, BUCKETS - 1)
                dve.wait_ge(trig, 2)
                dve.wait_ge(split_t, 2 * (sfill_of[("ckv", l, 0)] + 1))
                k1, k2 = mkv[:, :, KV_RANK:KV_RANK + HALF], mkv[:, :, KV_RANK + HALF:MKV]
                link(rope(k1, k2, k1, k2, [P, TILES, HALF]))
                dve.wait_ge(acc_act, acc_free[acc_of[("v", l)]][1])
                for t in range(TILES):
                    mark(nc.vector.tensor_copy(kfull[:, t, :, QK:MD], mkv[:, t, KV_RANK:MKV].unsqueeze(1).to_broadcast([P, MLA_HEADS, ROPE])))
                q4 = qfull[:].rearrange("p t (h d) -> p t h d", d=MD)
                q1, q2 = q4[:, :, :, QK:QK + HALF], q4[:, :, :, QK + HALF:MD]
                rope(q1, q2, q1, q2, [P, TILES, MLA_HEADS, HALF]).then_inc(roped, 1)
                attention(l)
                r = rms[("sub", l)]
                dve.wait_ge(rstd_ready, r + 1)
                for t in range(TILES):
                    v = o[:, t, 0:NB].rearrange("p (h d) -> p h d", h=DIFF_HEADS)
                    ins = nc.vector.tensor_tensor(v, v, rstd[:, r, 4 * t:4 * t + 4].unsqueeze(2).to_broadcast([P, DIFF_HEADS, P]), ALU.mult)
                ins.then_inc(xn_ready, 1)
                for i in range(4):
                    split_fill(("o", l, i), 2 * i, 2)
                dve_lo(dve, split_unit(H_WO[l] + 3))
                for nh in range(2):
                    q = acc_of[("wo", l, nh)]
                    if nh == 1:
                        for i in range(2):
                            dve_lo(dve, split_unit(H_WO[l] + 4 + i) if l == 0 else Unit(i, 0))
                    dve.wait_ge(unit_done, acc_last(("wo", l, nh)).done)
                    cs = slice(nh * NB, (nh + 1) * NB)
                    gated_add(gate_a, [(2 * (q % 2) + t, t, cs) for t in range(TILES)], WO_ADDED[l][nh])
                if l == 0:
                    dve_lo(dve, split_unit(H_WO[l] + 6))
                if l == 1:
                    link(nc.vector.tensor_copy(router_hi[:], col("router")))
                    nc.vector.tensor_tensor(router_lo[:], col("router"), router_hi[:].bitcast(F32), ALU.subtract).then_inc(router_split, 1)
                    nc.vector.tensor_copy(ident_b[:], ident).then_inc(router_split, 1)
                normalise_x(("f", l))
                for i in range(4):
                    split_fill(("f", l, i), 2 * i, 2)

            def gated_add(gate, parts, count):
                scaled = []
                before = count - len(parts)
                wait(dve, x_added, before)
                for i in range(len(parts) + 1):
                    if i < len(parts):
                        b, t, cs = parts[i]
                        if i >= 2:
                            dve.wait_ge(x_added, before + i - 1)
                        scaled.append(mark(nc.vector.tensor_tensor(tmp[:, i % 2, :], bank[b], gate[:, cs], ALU.mult)))
                    if i:
                        b, t, cs = parts[i - 1]
                        dve.wait_ge(dve_step, scaled[i - 1])
                        nc.vector.tensor_tensor(x[:, t, cs], x[:, t, cs], tmp[:, (i - 1) % 2, :], ALU.add).then_inc(x_added, 1)

            def act_part(j, tiles, base_s):
                for t in range(tiles):
                    dve.wait_ge(silu_done, base_s + (tiles * j + t + 1))
                    if t == 0:
                        wait(dve, aT_filled, (base_s if isinstance(base_s, int) else base_s - BLOCKS) + j)
                    b = bank[4 + t] if tiles == 2 else bank[2 + j % 2]
                    nc.vector.tensor_tensor(act_f[:, t, :], b[:, FB:2 * FB], silu[:, t, :], ALU.mult).then_inc(act_done, 1)

            def aT_lo_part(j, tiles, base_h):
                dve.wait_ge(aT_hi_ready, base_h + (j + 1))
                b = bank[6 if tiles == 2 else 4]
                w = 2 * P * tiles
                nc.vector.tensor_tensor(aT[tiles][1][:, j % 2, 0:w], b[:, 0:w], aT[tiles][0][:, j % 2, 0:w].bitcast(F32), ALU.subtract).then_inc(aT_lo_ready, 1)

            layer_attention(0)
            h0 = split_of[("A", 0)]
            for j in range(BLOCKS):
                if j:
                    aT_lo_part(j - 1, 2, 0)
                dve_lo(dve, split_unit(h0 + ffn_index[("A", j)] + 3))
                act_part(j, 2, 0)
                dve_lo(dve, split_unit(h0 + ffn_index[("B", j)] + 3))
                if j:
                    dve_lo(dve, split_unit(h0 + ffn_index[("C", j - 1)] + 3))
                if j < 10:
                    ada_take(12 + j)
            aT_lo_part(BLOCKS - 1, 2, 0)
            dve.wait_ge(unit_done, Unit(("C", BLOCKS - 1)).done)
            gated_add(gate_f, [(b, b // 2, slice((b % 2) * NB, (b % 2 + 1) * NB)) for b in range(4)], FFN_ADDED)
            layer_attention(1)

            dve.wait_ge(xn_part_ready, 1)
            nc.vector.tensor_tensor(xn_rest[:], xn[:], xn_part[0][:], ALU.subtract).then_inc(xn_part_ready, 1)
            dve.wait_ge(routed, 2)
            link(nc.vector.tensor_copy(rl[:].rearrange("p t e -> p (t e)"), bank[7][:, 0:TILES * EXPERTS]))
            for t in range(TILES):
                link(nc.vector.max(top_v[:, t, :], rl[:, t, :]))
                link(nc.vector.max_index(top_i[:, t, :], top_v[:, t, :], rl[:, t, :]))
            link(nc.vector.tensor_copy(top_f[:], top_i[:]))
            nc.vector.tensor_scalar(top_w[:, :, 0:1], top_v[:, :, 0:1], -1.0, None, ALU.mult).then_inc(chosen, 1)
            for t in range(TILES):
                for i in range(2):
                    mark(nc.vector.tensor_scalar(hot[:, t, i, :], iota[:, 0:EXPERTS], top_f[:, t, i:i + 1], None, ALU.is_equal))
            link(nc.vector.memset(sel_t[:], 0.0))
            link(nc.vector.tensor_tensor(sel_t[:, :, 0:EXPERTS], hot[:, :, 0, :], hot[:, :, 1, :], ALU.add))
            nc.vector.memset(pos_t[:], 0.0).then_inc(chosen, 1)
            dve.wait_ge(xn_part_ready, 3)
            nc.vector.tensor_tensor(xn_part[2][:], xn_rest[:], xn_part[1][:], ALU.subtract).then_inc(xn_part_ready, 1)
            dve.wait_ge(placed_ps, 1)
            link(nc.vector.tensor_copy(pos_t[:, :, 0:EXPERTS], bank[7][:, 0:16].rearrange("p (t e) -> p t e", t=TILES)))
            link(nc.vector.tensor_copy(count[:], bank[7][:, 16:24]))

            def build_slots(p):
                for t in range(TILES):
                    ins = nc.vector.tensor_scalar(slot_of[:, t, :], iota, pos_t[:, t, bass.ds(p, 1)], sel_t[:, t, bass.ds(p, 1)],
                                                  ALU.is_equal, ALU.mult)
                ins.then_inc(slots_built, 1)

            build_slots(0)
            link(nc.vector.memset(gate_t[:], 0.0))
            dve.wait_ge(top_exp, 2)
            link(nc.vector.tensor_scalar(top_w[:, :, 2:3], top_w[:, :, 1:2], 1.0, None, ALU.add))
            link(nc.vector.reciprocal(top_w[:, :, 2:3], top_w[:, :, 2:3]))
            link(nc.vector.tensor_tensor(top_w[:, :, 3:4], top_w[:, :, 1:2], top_w[:, :, 2:3], ALU.mult))
            for t in range(TILES):
                gates = gate_t[:, t, 1:1 + EXPERTS]
                link(nc.vector.tensor_scalar(gates, hot[:, t, 0, :], top_w[:, t, 2:3], None, ALU.mult))
                link(nc.vector.scalar_tensor_tensor(gates, hot[:, t, 1, :], top_w[:, t, 3:4], gates, ALU.mult, ALU.add))
            mark(nc.vector.memset(rank[:, 0:1], 0.0))
            link(nc.vector.tensor_scalar(over[:], count[:], float(SLOTS), None, ALU.is_gt))
            for e in range(EXPERTS):
                link(nc.vector.tensor_tensor(rank[:, e + 1:e + 2], rank[:, e:e + 1], over[:, e:e + 1], ALU.add))
            link(nc.vector.memset(pass_f[:], 0.0))
            mark(nc.vector.tensor_copy(pass_f[:, 0:EXPERTS], iota[:, 0:EXPERTS]))
            mark(nc.vector.tensor_scalar(pass_f[:, MAX_PASS + 1:MAX_PASS + 2], rank[:, EXPERTS:EXPERTS + 1], float(EXPERTS), None, ALU.add))
            for i in range(MAX_OVER):
                mark(nc.vector.scalar_tensor_tensor(over_hot[:, i, :], rank[:, 0:EXPERTS], float(i), over[:], ALU.is_equal, ALU.mult))
            dve.wait_ge(dve_step, steps_done[0])
            for i in range(MAX_OVER):
                c = EXPERTS + i
                picks = [(pass_f[:, c:c + 1], iota[:, 0:EXPERTS])]
                for t in range(TILES):
                    picks += [(sel_t[:, t, c:c + 1], sel_t[:, t, 0:EXPERTS]), (gate_t[:, t, 1 + c:2 + c], gate_t[:, t, 1:1 + EXPERTS]),
                              (pos_t[:, t, c:c + 1], pos_t[:, t, 0:EXPERTS])]
                for k, (dst, src) in enumerate(picks):
                    mark(nc.vector.tensor_tensor_reduce(out=picked[:, i, k, :], in0=over_hot[:, i, :], in1=src, scale=1.0, scalar=0.0,
                                                        op0=ALU.mult, op1=ALU.add, accum_out=dst))
            dve.wait_ge(dve_step, steps_done[0])
            link(nc.vector.tensor_scalar(pos_t[:, :, EXPERTS:MAX_PASS], pos_t[:, :, EXPERTS:MAX_PASS], float(SLOTS), None, ALU.subtract))
            nc.vector.tensor_copy(pass_i[:], pass_f[:]).then_inc(tables, 1)

            def split_gathered(base):
                dve.wait_ge(xg_evac, base * 2 + 2)
                nc.vector.tensor_copy(xg_hi[:], xg32[:]).then_inc(xg_split, 1)
                dve.wait_ge(xg_split, base * 2 + 1)
                nc.vector.tensor_tensor(xg_lo[:], xg32[:], xg_hi[:].bitcast(F32), ALU.subtract).then_inc(xg_split, 1)

            def add_results(p, first, end):
                for i in range(first, end):
                    t, cs = i // 2, slice((i % 2) * NB, (i % 2 + 1) * NB)
                    dve.wait_ge(scattered, p * 4 + (i + 1))
                    nc.vector.scalar_tensor_tensor(moe_out[:, t, cs], bank[5 + i % 3], gate_t[:, t, bass.ds(p, 1)], moe_out[:, t, cs],
                                                   ALU.mult, ALU.add).then_inc(moe_added, 1)

            split_gathered(0)
            dve.wait_ge(tables, 1)
            n_pass = dve.value_load(pass_i[0:1, MAX_PASS + 1:MAX_PASS + 2], min_val=EXPERTS, max_val=MAX_PASS)
            with dve.Fori(0, n_pass) as p:
                base_h = p * BLOCKS + BLOCKS
                base_s = p * BLOCKS + 2 * BLOCKS
                dve_lo(dve, Unit(2, p))
                for j in range(BLOCKS):
                    if j:
                        aT_lo_part(j - 1, 1, base_h)
                    if ffn_index[("A", j)] + 3 < UPP:
                        dve_lo(dve, Unit(ffn_index[("A", j)] + 3, p))
                    if j in (2, 3):
                        add_results(p, 2 * j - 4, 2 * j - 2)
                    act_part(j, 1, base_s)
                    if ffn_index[("B", j)] + 3 < UPP:
                        dve_lo(dve, Unit(ffn_index[("B", j)] + 3, p))
                    if j and ffn_index[("C", j - 1)] + 3 < UPP:
                        dve_lo(dve, Unit(ffn_index[("C", j - 1)] + 3, p))
                    if j == 5:
                        dve.wait_ge(token_filled, p + 1)
                        build_slots(p + 1)
                split_gathered(p + 1)
                aT_lo_part(BLOCKS - 1, 1, base_h)
                for r in range(2):
                    dve_lo(dve, Unit(UPP + r, p))
                for b in range(2):
                    dve.wait_ge(y_hi_ready, p * 2 + (b + 3))
                    cs = slice(b * NB, (b + 1) * NB)
                    nc.vector.tensor_tensor(y_lo[:, cs], bank[b], y_hi[:, cs].bitcast(F32), ALU.subtract).then_inc(y_lo_ready, 1)
            add_results(n_pass, 0, 4)
            dve.wait_ge(moe_added, n_pass * 4 + 4)
            for t in range(TILES):
                link(nc.vector.tensor_tensor(moe_out[:, t, :], moe_out[:, t, :], gate_f[:], ALU.mult))
                nc.vector.tensor_tensor(x[:, t, :], x[:, t, :], moe_out[:, t, :], ALU.add).then_inc(moe_in_x, 1)
            r = rms[("final", 1)]
            dve.wait_ge(rstd_ready, r + 1)
            dve.wait_ge(gate_a_row, 48)
            for t in range(TILES):
                nc.vector.scalar_tensor_tensor(xn[:, t, :], x[:, t, :], rstd[:, r, t:t + 1], gate_a[:], ALU.mult, ALU.mult).then_inc(final_ready, 1)

        @block.tensor
        def _(pe):
            def products(dst, first, last, hi, lo, u, cs):
                wh, wl = w_hi[:, u.hi_slot, u.hi_cols(cs)], w_lo[:, u.slot, cs]
                nc.tensor.matmul(dst, hi, wh, start=first, stop=False)
                nc.tensor.matmul(dst, hi, wl, start=False, stop=False)
                return nc.tensor.matmul(dst, lo, wh, start=False, stop=last)

            def chunk(c, t):
                ts = slice(t * P, (t + 1) * P)
                return TH[:, c, ts], TL[:, c, ts]

            def ada_unit(G, kh):
                l, g = ada_groups[G]
                u = Unit(("ada", l, g, kh))
                pe.wait_ge(raw_loaded[u.slot], u.loaded)
                if kh == 0:
                    wait(pe, ada_used, G)
                for k in range(4):
                    ins = nc.tensor.matmul(ADA[32 * k:32 * k + 32, :], cond_rep[:, 4 * kh + k, :], raw[:, u.slot, k * NB:(k + 1) * NB],
                                           start=(kh == 0), stop=(kh == 1), tile_position=(0, 32 * k))
                ins.then_inc(unit_done, 1)

            def ada_combine(G):
                l, g = ada_groups[G]
                pe.wait_ge(ada_part, G + 1)
                if g in (4, 5, 10, 11):
                    ins = nc.tensor.matmul(ADA, const("selrow"), ada_p[:, G % 2, :], start=True, stop=True)
                else:
                    for c in range(4):
                        ins = nc.tensor.matmul(ADA[:, c:c + 1], ada_p[:, G % 2, c * P:(c + 1) * P], const("selrow")[:, 0:1], start=True, stop=True)
                ins.then_inc(ada_comb, 1)

            def fill(name, blocks):
                f = fill_of[name]
                wait(pe, evacuated, f - 2)
                for i, (src, rows) in enumerate(blocks):
                    ins = nc.tensor.transpose(bank[4 + f % 3][0:rows, i * P:(i + 1) * P], src, ident)
                ins.then_inc(filled, 1)

            def fill_tokens(kind, l, src, chunks):
                for i in range((chunks + 1) // 2):
                    cs = [c for c in (2 * i, 2 * i + 1) if c < chunks]
                    fill((kind, l, i), [(src(t, c), P) for c in cs for t in range(TILES)])

            def wait_chunk(kind, l, c):
                if c % 2 == 0:
                    pe.wait_ge(split_t, 2 * (sfill_of[(kind, l, c // 2)] + 1))

            def run_group(group, units, chunks_of, width, kind=None):
                q = acc_of[group]
                if q >= 2:
                    s, v = acc_free[q - 2]
                    pe.wait_ge(s, v)
                for i, u in enumerate(units):
                    cks = chunks_of[i]
                    for k, c in enumerate(cks):
                        if k in (0, 2):
                            pe.wait_ge(lo_ready, u.ready[k // 2])
                        if kind:
                            wait_chunk(kind, group[1], c)
                        for t in range(TILES):
                            hi, lo = chunk(c, t)
                            ins = products(bank[2 * (q % 2) + t][:, 0:width], i == 0 and k == 0, i == len(units) - 1 and k == len(cks) - 1,
                                           hi, lo, u, slice(k * width, (k + 1) * width))
                        if k in (1, len(cks) - 1):
                            ins.then_inc(unit_done, 1)

            def attention(l):
                def score(s):
                    S = NS * l + s
                    kind, hp, t, m = steps[s]
                    n = n_keys(s)
                    if s >= 3:
                        pe.wait_ge(soft, 2 * (S - 3) + 1)
                    for hh in range(2):
                        dst = bank[s % 3][:, hh * SEQ:hh * SEQ + n]
                        if kind == "diff":
                            rows = slice(QK * m, QK * (m + 1))
                            q_, k_ = dT[rows, 0, hp, :], dT[rows, 1, hp, :]
                        else:
                            q_, k_ = mT[0:MD, 0, hp, :], mT[0:MD, 1, hp, :]
                        ins = nc.tensor.matmul(dst, q_[:, hh * SEQ + t * P:hh * SEQ + (t + 1) * P], k_[:, hh * SEQ:hh * SEQ + n],
                                               start=True, stop=True)
                    ins.then_inc(scored, 1)

                def transpose_probs(s):
                    S = NS * l + s
                    pe.wait_ge(exped, 2 * (S + 1))
                    if s >= 2:
                        pe.wait_ge(pT_ready, S - 1)
                    kb = n_keys(s) // P
                    for hh in range(2):
                        for k in range(kb):
                            i = hh * kb + k
                            ins = nc.tensor.transpose(bank[3 + s % 2][:, i * P:(i + 1) * P], probs[:, s % 3, hh, k * P:(k + 1) * P], ident)
                    ins.then_inc(pT_filled, 1)

                def values(s):
                    S = NS * l + s
                    kind, hp, t, m = steps[s]
                    pe.wait_ge(pT_ready, S + 1)
                    if s >= 2:
                        pe.wait_ge(o_ready, S - 1)
                    kb = n_keys(s) // P
                    dvw = P if kind == "diff" else QK
                    v = dv if kind == "diff" else vm
                    for hh in range(2):
                        h = 2 * hp + hh
                        for k in range(kb):
                            i = hh * kb + k
                            ins = nc.tensor.matmul(bank[5 + s % 2][:, hh * dvw:(hh + 1) * dvw], pT[s % 2][:, i * P:(i + 1) * P],
                                                   v[:, k, h * dvw:(h + 1) * dvw], start=(k == 0), stop=(k == kb - 1))
                    ins.then_inc(pv_done, 1)

                first = 4 if l == 0 else 22
                n_ada = 8 if l == 0 else 2
                pe.wait_ge(acc_act, acc_free[acc_of[("v", l)]][1])
                pe.wait_ge(evacuated, fill_of[("mT", l, 1, 3)] + 1)
                for s in range(NS + 3):
                    if s < NS:
                        score(s)
                    if s >= 2 and s % 2 == 0 and s // 2 <= n_ada:
                        ada_combine(first + s // 2 - 1)
                    if 2 <= s < NS + 2:
                        transpose_probs(s - 2)
                    if s >= 3:
                        values(s - 3)
                    if s < 2 * n_ada:
                        G = first + s // 2
                        ada_unit(G, s % 2)

            def layer_attention(l):
                pe.wait_ge(xn_ready, rms[("h", l)] + 1)
                fill_tokens("h", l, lambda t, c: xn[:, t, c * P:(c + 1) * P], KC)
                for gi, (_, _, w) in enumerate(IN_GROUPS):
                    run_group(("in", l, gi), [Unit(("in", l, gi, kh)) for kh in range(2)], [range(4), range(4, 8)], w,
                              None if gi else "h")
                pe.wait_ge(xn_ready, rms[("lat", l)] + 1)
                fill_tokens("mq", l, lambda t, c: mq[:, t, c * P:(c + 1) * P], 3)
                fill_tokens("ckv", l, lambda t, c: mkv[:, t, c * P:(c + 1) * P], 2)
                pe.wait_ge(acc_act, acc_free[acc_of[("in", l, 4)]][1])
                for qk, src in ((0, dq), (1, dk)):
                    for hp in range(2):
                        fill(("dT", l, qk, hp), [(src[:, t, (2 * hp + hh) * P:(2 * hp + hh + 1) * P], P) for hh in range(2) for t in range(TILES)])
                for u in range(2):
                    run_group(("uq", l, u), [Unit(("uq", l, u))], [range(3)], 384, None if u else "mq")
                pe.wait_ge(split_t, 2 * (sfill_of[("ckv", l, 0)] + 1))
                u = Unit(("ukv", l))
                for n, name in enumerate(("kn", "v")):
                    q = acc_of[(name, l)]
                    pe.wait_ge(*acc_free[q - 2])
                    for k in range(2):
                        pe.wait_ge(lo_ready, u.ready[k])
                        for t in range(TILES):
                            hi, lo = chunk(4 + k, t)
                            off = k * D + n * NB
                            ins = products(bank[2 * (q % 2) + t], k == 0, k == 1, hi, lo, u, slice(off, off + NB))
                        if n == 1:
                            ins.then_inc(unit_done, 1)
                    if n == 0:
                        ins.then_inc(kn_done, 1)
                pe.wait_ge(roped, l + 1)
                for qk in range(2):
                    for hp in range(4):
                        def src(t, h):
                            return qfull[:, t, h * MD:(h + 1) * MD] if qk == 0 else kfull[:, t, h, :]
                        fill(("mT", l, qk, hp), [(src(t, 2 * hp + hh), MD) for hh in range(2) for t in range(TILES)])
                attention(l)
                pe.wait_ge(o_ready, NS * (l + 1))
                pe.wait_ge(xn_ready, rms[("sub", l)] + 1)
                fill_tokens("o", l, lambda t, c: o[:, t, c * P:(c + 1) * P], KC)
                for nh in range(2):
                    run_group(("wo", l, nh), [Unit(("wo", l, nh, kh)) for kh in range(2)], [range(4), range(4, 8)], NB,
                              None if nh else "o")
                pe.wait_ge(xn_ready, rms[("f", l)] + 1)
                fill_tokens("f", l, lambda t, c: xn[:, t, c * P:(c + 1) * P], KC)

            def up_half(j, kh, tiles, u, stationary, base_s):
                if kh == 0:
                    wait(pe, act_done, base_s + (2 * j if tiles == 2 else j - 1))
                for k in range(4):
                    if k in (0, 2):
                        pe.wait_ge(lo_ready, u.ready[k // 2])
                    if j == 0 and tiles == 2:
                        wait_chunk("f", 0, 4 * kh + k)
                    for t in range(tiles):
                        hi, lo = stationary(4 * kh + k, t)
                        b = bank[4 + t] if tiles == 2 else bank[2 + j % 2]
                        ins = products(b, kh == 0 and k == 0, kh == 1 and k == 3, hi, lo, u, slice(k * NB, (k + 1) * NB))
                    if k in (1, 3):
                        ins.then_inc(unit_done, 1)

            def transpose_act(j, tiles, base_s, base_h):
                pe.wait_ge(act_done, base_s + tiles * (j + 1))
                wait(pe, aT_lo_ready, base_h + j)
                b = bank[6 if tiles == 2 else 4]
                for c in range(2):
                    for t in range(tiles):
                        i = c * tiles + t
                        ins = nc.tensor.transpose(b[:, i * P:(i + 1) * P], act_f[:, t, c * P:(c + 1) * P], ident)
                ins.then_inc(aT_filled, 1)

            def down(j, tiles, u, base_h, then=None):
                pe.wait_ge(aT_lo_ready, base_h + (j + 1))
                for c in range(2):
                    pe.wait_ge(lo_ready, u.ready[c])
                    for t in range(tiles):
                        i = c * tiles + t
                        hi, lo = aT[tiles][0][:, j % 2, i * P:(i + 1) * P], aT[tiles][1][:, j % 2, i * P:(i + 1) * P]
                        for half in range(2):
                            ins = products(bank[2 * t + half], j == 0 and c == 0, j == BLOCKS - 1 and c == 1, hi, lo, u,
                                           slice(c * D + half * NB, c * D + (half + 1) * NB))
                    ins.then_inc(unit_done, 1)
                    if then and c == 0:
                        then()

            pe.wait_ge(cond_ready, 1)
            for G in range(4):
                for kh in range(2):
                    ada_unit(G, kh)
                ada_combine(G)
            layer_attention(0)
            pe.wait_ge(x_added, WO_ADDED[0][1])
            pe.wait_ge(evacuated, fill_of[("f", 0, 3)] + 1)
            for j in range(BLOCKS):
                up_half(j, 0, 2, Unit(("A", j)), chunk, 0)
                if j:
                    transpose_act(j - 1, 2, 0, 0)
                up_half(j, 1, 2, Unit(("B", j)), chunk, 0)
                if j:
                    down(j - 1, 2, Unit(("C", j - 1)), 0,
                         then=(lambda: transpose_act(BLOCKS - 1, 2, 0, 0)) if j == BLOCKS - 1 else None)
                if j < 10:
                    for kh in range(2):
                        ada_unit(12 + j, kh)
                    ada_combine(12 + j)
            down(BLOCKS - 1, 2, Unit(("C", BLOCKS - 1)), 0)
            pe.wait_ge(x_added, FFN_ADDED)
            layer_attention(1)

            pe.wait_ge(router_split, 2)
            for c in range(KC):
                wait_chunk("f", 1, c)
                rh, rlo = router_hi[:, c * EXPERTS:(c + 1) * EXPERTS], router_lo[:, c * EXPERTS:(c + 1) * EXPERTS]
                dst = bank[7][0:EXPERTS, 0:SEQ]
                nc.tensor.matmul(dst, rh, TH[:, c, :], start=(c == 0), stop=False)
                nc.tensor.matmul(dst, rlo, TH[:, c, :], start=False, stop=False)
                ins = nc.tensor.matmul(dst, rh, TL[:, c, :], start=False, stop=(c == KC - 1))
            ins.then_inc(routed, 1)
            pe.wait_ge(logits_copied, 1)
            for t in range(TILES):
                ins = nc.tensor.transpose(bank[7][:, t * EXPERTS:(t + 1) * EXPERTS], logits[0:EXPERTS, t * P:(t + 1) * P],
                                          ident[0:EXPERTS, 0:EXPERTS])
            ins.then_inc(routed, 1)
            pe.wait_ge(chosen, 2)
            sel = [sel_t[:, t, 0:EXPERTS] for t in range(TILES)]
            nc.tensor.matmul(bank[7][:, 0:8], const("before"), sel[0], start=True, stop=True)
            nc.tensor.matmul(bank[7][:, 8:16], const("before"), sel[1], start=True, stop=False)
            nc.tensor.matmul(bank[7][:, 8:16], ones[:], sel[0], start=False, stop=True)
            nc.tensor.matmul(bank[7][:, 16:24], ones[:], sel[0], start=True, stop=False)
            nc.tensor.matmul(bank[7][:, 16:24], ones[:], sel[1], start=False, stop=True).then_inc(placed_ps, 1)

            def gather(base):
                pe.wait_ge(slots_built, base + 1)
                for b in range(2):
                    for c in range(4 * b, 4 * b + 4):
                        dst = bank[5 + b][:, (c % 4) * P:(c % 4 + 1) * P]
                        for n, (t, part) in enumerate((t, part) for t in range(TILES) for part in xn_part):
                            ins = nc.tensor.matmul(dst, part[:, t, c * P:(c + 1) * P], slot_of[:, t, :], start=(n == 0), stop=(n == 5))
                    ins.then_inc(gathered, 1)

            def scatter(p, first, end):
                pe.wait_ge(y_lo_ready, p * 2 + 2)
                pe.wait_ge(token_ready, p + 1)
                for i in range(first, end):
                    t, cs = i // 2, slice((i % 2) * NB, (i % 2 + 1) * NB)
                    dst = bank[5 + i % 3]
                    if i == 3:
                        pe.wait_ge(moe_added, p * 4 + 1)
                    nc.tensor.matmul(dst, token_of[:, t * P:(t + 1) * P], y_hi[:, cs], start=True, stop=False)
                    nc.tensor.matmul(dst, token_of[:, t * P:(t + 1) * P], y_lo[:, cs], start=False, stop=True).then_inc(scattered, 1)

            def slots_chunk(c, t):
                return xg_hi[:, c, :], xg_lo[:, c, :]

            gather(0)
            pe.wait_ge(tables, 1)
            n_pass = pe.value_load(pass_i[0:1, MAX_PASS + 1:MAX_PASS + 2], min_val=EXPERTS, max_val=MAX_PASS)
            with pe.Fori(0, n_pass) as p:
                base_h = p * BLOCKS + BLOCKS
                base_s = p * BLOCKS + 2 * BLOCKS
                pe.wait_ge(xg_split, p * 2 + 2)
                for j in range(BLOCKS):
                    up_half(j, 0, 1, Unit(ffn_index[("A", j)], p), slots_chunk, base_s)
                    if j:
                        transpose_act(j - 1, 1, base_s, base_h)
                    up_half(j, 1, 1, Unit(ffn_index[("B", j)], p), slots_chunk, base_s)
                    if j:
                        down(j - 1, 1, Unit(ffn_index[("C", j - 1)], p), base_h,
                             then=(lambda: transpose_act(BLOCKS - 1, 1, base_s, base_h)) if j == BLOCKS - 1 else None)
                    if j in (1, 2):
                        scatter(p, 2 * j - 2, 2 * j)
                    if j == 4:
                        pe.wait_ge(moe_added, p * 4 + 3)
                        for t in range(TILES):
                            ins = nc.tensor.matmul(bank[7][:, t * P:(t + 1) * P], slot_of[:, t, :], ident_b[:], start=True, stop=True)
                        ins.then_inc(token_filled, 1)
                    if j == 7:
                        pe.wait_ge(moe_added, p * 4 + 4)
                        gather(p + 1)
                down(BLOCKS - 1, 1, Unit(ffn_index[("C", BLOCKS - 1)], p), base_h)
            scatter(n_pass, 0, 4)


def _chunks(w, width):
    k, n = w.shape
    return w.reshape(k // P, P, n).transpose(1, 0, 2).reshape(P, -1)


def _ffn_units(w1, w3, w2, np):
    out = []
    for kind, j in ffn_order():
        if kind == "C":
            out.append(_chunks(w2[j * FB:(j + 1) * FB], D))
        else:
            rows = slice(0, D // 2) if kind == "A" else slice(D // 2, D)
            cs = slice(j * FB, (j + 1) * FB)
            out.append(_chunks(np.concatenate([w1[rows, cs], w3[rows, cs]], axis=1), NB))
    return out


def _pack(inputs, np):
    f = {k: np.ascontiguousarray(v) for k, v in inputs.items()}
    ffn = dict(zip(ffn_order(), _ffn_units(f["ffn_w1"][0], f["ffn_w3"][0], f["ffn_w2"][0], np)))
    ukv_order = np.arange(MLA_HEADS * 2 * QK).reshape(MLA_HEADS, 2, QK).transpose(1, 0, 2).reshape(-1)
    parts = []
    for name, _, _ in static_units():
        kind = name[0]
        if kind == "ada":
            _, l, g, kh = name
            w = _chunks(f["w_ada"][l][kh * 512:(kh + 1) * 512, g * NB:(g + 1) * NB], NB)
        elif kind == "in":
            _, l, gi, kh = name
            _, c0, width = IN_GROUPS[gi]
            w = _chunks(f["w_in"][l][kh * 512:(kh + 1) * 512, c0:c0 + width], width)
        elif kind == "uq":
            _, l, u = name
            w = _chunks(f["w_uq"][l][:, u * 384:(u + 1) * 384], 384)
        elif kind == "ukv":
            w = _chunks(f["w_ukv"][name[1]][:, ukv_order], D)
        elif kind == "wo":
            _, l, nh, kh = name
            w = _chunks(f["w_o"][l][kh * 512:(kh + 1) * 512, nh * NB:(nh + 1) * NB], NB)
        else:
            w = ffn[name]
        parts.append(w.reshape(-1))
    w_static = np.concatenate(parts)
    w_moe = np.stack([np.stack(_ffn_units(f["moe_w1"][0, e], f["moe_w3"][0, e], f["moe_w2"][0, e], np)) for e in range(EXPERTS)])

    def columns(v):
        return v.reshape(-1, P).T

    cols = np.concatenate([columns(f["g_attn"]), columns(f["g_ffn"]), columns(f["b_ada"]), columns(f["mla_q_norm"]),
                           columns(f["mla_kv_norm"]), columns(f["diff_subln_g"]), columns(f["c"]),
                           _chunks(f["moe_router"][0], EXPERTS)], axis=1)
    r = np.arange(P)
    causal = np.where(r[:, None] >= r[None, :], 0.0, MASKED)
    freq = np.power(np.float32(THETA), -np.arange(HALF, dtype=np.float32) / np.float32(HALF))
    consts = np.concatenate([
        np.eye(P), causal, np.zeros((P, P)), causal,
        r[:, None] < r[None, :],
        np.repeat((r % 32 == 0)[:, None], P, axis=1),
        np.repeat(r[None, :], P, axis=0),
        np.repeat(freq[None, :], P, axis=0)], axis=1).astype(np.float32)
    return {
        "x": f["x"], "positions": f["positions"], "pos_cols": np.ascontiguousarray(columns(f["positions"])),
        "consts": consts, "cols": np.ascontiguousarray(cols),
        "b_ada": f["b_ada"], "rel_bias": f["rel_bias"], "diff_lambda": f["diff_lambda"], "g_final": f["g_final"],
        "w_static": w_static, "w_moe": w_moe,
    }


def kernel(**inputs):
    import numpy as _np
    import concourse.bacc as _bacc
    from concourse import mybir as _mybir
    from concourse.bass_utils import run_bass_kernel_spmd as _run

    nc = _bacc.Bacc("TRN2", target_bir_lowering=False, num_devices=1, dynamic_dma_scratch_size=1024)
    arrays, args = {}, []
    for name, a in _pack({k: _np.asarray(v) for k, v in inputs.items()}, _np).items():
        arrays[f"in_{name}"] = a
        args.append(nc.dram_tensor(f"in_{name}", a.shape, _mybir.dt.from_np(a.dtype), kind="ExternalInput").ap())
    out = nc.dram_tensor("out", (1, SEQ, D), F32, kind="ExternalOutput").ap()
    build(nc, *args, out)
    return _run(nc, [arrays], core_ids=[0]).results[0]["out"]
```
